# Optimizing a Trainium2 kernel written in Bass

```python
import math
import jax
import jax.numpy as jnp
from jax import lax
import numpy as np

D_MODEL = 1024
BATCH = 1
SEQ = 512
DEPTH = 2
DEC_BATCH = 8
DEC_SEQ = 1
PAST_LEN = 1024
PAGE_SIZE = 128

N_MIXERS = 2
N_A_LAYERS = (DEPTH + 1) // 2
N_B_LAYERS = DEPTH // 2
D_FF = 2816
CHUNK = 128
D_GMLP = 2 * D_MODEL
N_GROUPS_A = 8
GROUP_DIM_A = D_GMLP // N_GROUPS_A
N_HEADS = 16
Q_LORA = 256
KV_LORA = 128
NOPE_DIM = 128
ROPE_DIM = 64
QK_DIM = NOPE_DIM + ROPE_DIM
V_DIM = 128
CACHE_DIM = KV_LORA + ROPE_DIM + N_HEADS
ROPE_THETA = 10000.0
Q_BLOCK = 128
EPS = 1e-6
NEG_INF = -1e30

kernel_name = 'macaron_gmlp_mla_hybrid_step'

def rms_norm(x, g):
    xf = x.astype(jnp.float32)
    y = xf * lax.rsqrt(jnp.mean(xf * xf, axis=-1, keepdims=True) + EPS)
    return (y * g.astype(jnp.float32)).astype(x.dtype)

def swiglu(h, w_gate, w_up, w_down):
    return (jax.nn.silu(h @ w_gate) * (h @ w_up)) @ w_down

def rope(x, pos):
    half = ROPE_DIM // 2
    inv = ROPE_THETA ** (-jnp.arange(half, dtype=jnp.float32) / half)
    ang = pos.astype(jnp.float32)[:, None] * inv[None, :]
    cos = jnp.cos(ang)[None, :, None, :].astype(x.dtype)
    sin = jnp.sin(ang)[None, :, None, :].astype(x.dtype)
    x1, x2 = x[..., :half], x[..., half:]
    return jnp.concatenate([x1 * cos - x2 * sin, x1 * sin + x2 * cos], axis=-1)

def chunk_spatial_mix(v, w_s, b_s):
    bsz, s_len, _ = v.shape
    mask = jnp.tril(jnp.ones((CHUNK, CHUNK), dtype=bool))
    w = jnp.where(mask[None], w_s, 0.0).astype(v.dtype)
    b = b_s.astype(v.dtype)
    if s_len < CHUNK:
        w = w[:, :s_len, :s_len]
        b = b[:, :s_len]
        blk, pad = s_len, 0
    else:
        blk, pad = CHUNK, (-s_len) % CHUNK
    vp = jnp.pad(v, ((0, 0), (0, pad), (0, 0))) if pad else v
    n_chunks = vp.shape[1] // blk
    vc = vp.reshape(bsz, n_chunks, blk, N_GROUPS_A, GROUP_DIM_A)
    s = jnp.einsum('gij,bcjgd->bcigd', w, vc) + b.T[None, None, :, :, None]
    return s.reshape(bsz, n_chunks * blk, D_GMLP)[:, :s_len]

def gmlp_mixer(h, w_in, b_in, v_gain, w_s, b_s, w_out):
    z = jax.nn.gelu(h @ w_in + b_in)
    u, v = z[..., :D_GMLP], z[..., D_GMLP:]
    v = rms_norm(v, v_gain)
    s = chunk_spatial_mix(v, w_s, b_s)
    return (u * s) @ w_out, v

def mla_project(h, pos, w_dq, q_gain, w_uq, w_dkv, kv_gain, w_uk, qk_gain_q, qk_gain_k):
    cq = rms_norm(h @ w_dq, q_gain)
    q = jnp.einsum('bsr,rhd->bshd', cq, w_uq)
    q = jnp.concatenate([q[..., :NOPE_DIM], rope(q[..., NOPE_DIM:], pos)], axis=-1)
    q = rms_norm(q, qk_gain_q) * qk_gain_k.astype(q.dtype)
    q_lat = jnp.einsum('bshn,chn->bshc', q[..., :NOPE_DIM], w_uk)
    q_rope = q[..., NOPE_DIM:]
    ckv = h @ w_dkv
    c = rms_norm(ckv[..., :KV_LORA], kv_gain)
    k_rope = rope(ckv[:, :, None, KV_LORA:], pos)[:, :, 0]
    k_nope = jnp.einsum('bsc,chn->bshn', c, w_uk).astype(jnp.float32)
    ssq = jnp.sum(k_nope * k_nope, axis=-1) + jnp.sum(jnp.square(k_rope.astype(jnp.float32)), axis=-1)[..., None]
    k_scale = lax.rsqrt(ssq / QK_DIM + EPS).astype(h.dtype)
    rows = jnp.concatenate([c, k_rope, k_scale], axis=-1)
    return q_lat, q_rope, rows

def mla_attend(q_lat, q_rope, q_pos, keys, k_pos, w_uv, w_o):
    c = keys[..., :KV_LORA]
    kr = keys[..., KV_LORA:KV_LORA + ROPE_DIM]
    ks = jnp.transpose(keys[..., KV_LORA + ROPE_DIM:], (0, 2, 1)).astype(jnp.float32)
    bsz, s_q = q_lat.shape[:2]
    blk = Q_BLOCK if s_q % Q_BLOCK == 0 else s_q
    n_blk = s_q // blk
    scale = QK_DIM ** -0.5

    def block(args):
        ql, qr, qp = args
        s = (jnp.einsum('bqhc,bkc->bhqk', ql, c, preferred_element_type=jnp.float32)
             + jnp.einsum('bqhr,bkr->bhqk', qr, kr, preferred_element_type=jnp.float32))
        s = s * ks[:, :, None, :] * scale
        s = jnp.where(k_pos[None, None, None, :] <= qp[None, None, :, None], s, NEG_INF)
        p = jax.nn.softmax(s, axis=-1).astype(c.dtype)
        return jnp.einsum('bhqk,bkc->bqhc', p, c)

    ql_b = jnp.swapaxes(q_lat.reshape(bsz, n_blk, blk, N_HEADS, KV_LORA), 0, 1)
    qr_b = jnp.swapaxes(q_rope.reshape(bsz, n_blk, blk, N_HEADS, ROPE_DIM), 0, 1)
    qp_b = q_pos.reshape(n_blk, blk)
    o = lax.map(block, (ql_b, qr_b, qp_b))
    o = jnp.swapaxes(o, 0, 1).reshape(bsz, s_q, N_HEADS, KV_LORA)
    o = jnp.einsum('bshc,chv->bshv', o, w_uv).reshape(bsz, s_q, N_HEADS * V_DIM)
    return o @ w_o

def setup_inputs(seed: int = 0) -> dict:
    key = jax.random.key(seed)
    ks = jax.random.split(key, 32)
    f32 = jnp.float32

    def nrm(k, shape, fan_in):
        return jax.random.normal(k, shape, f32) * (fan_in ** -0.5)

    def gain(k, shape):
        return 1.0 + 0.1 * jax.random.normal(k, shape, f32)

    n_pages = PAST_LEN // PAGE_SIZE
    n_used = DEC_BATCH * n_pages
    n_pool = n_used + n_used // 4
    x_prompt = jax.random.normal(ks[0], (BATCH, SEQ, D_MODEL), f32)
    x_sample = jax.random.normal(ks[1], (DEC_BATCH, DEC_SEQ, D_MODEL), f32)
    z = jax.random.normal(ks[2], (N_B_LAYERS, n_pool, PAGE_SIZE, CACHE_DIM), f32)
    is_scale_col = jnp.arange(CACHE_DIM) >= KV_LORA + ROPE_DIM
    cache_mla = jnp.where(is_scale_col, 1.0 + 0.3 * jnp.tanh(z), z)
    page_table = jax.random.permutation(ks[3], n_pool)[:n_used].reshape(DEC_BATCH, n_pages).astype(jnp.int32)
    return {
        'x_prompt': x_prompt,
        'x_sample': x_sample,
        'cache_mla': cache_mla,
        'page_table': page_table,
        'norm_g': gain(ks[4], (DEPTH, 3, D_MODEL)),
        'ffn_w_gate': nrm(ks[5], (DEPTH, 2, D_MODEL, D_FF), D_MODEL),
        'ffn_w_up': nrm(ks[6], (DEPTH, 2, D_MODEL, D_FF), D_MODEL),
        'ffn_w_down': nrm(ks[7], (DEPTH, 2, D_FF, D_MODEL), D_FF),
        'gmlp_w_in': nrm(ks[8], (N_A_LAYERS, D_MODEL, 2 * D_GMLP), D_MODEL),
        'gmlp_b_in': 0.02 * jax.random.normal(ks[9], (N_A_LAYERS, 2 * D_GMLP), f32),
        'gmlp_v_norm': gain(ks[10], (N_A_LAYERS, D_GMLP)),
        'gmlp_w_s': nrm(ks[11], (N_A_LAYERS, N_GROUPS_A, CHUNK, CHUNK), CHUNK),
        'gmlp_b_s': gain(ks[12], (N_A_LAYERS, N_GROUPS_A, CHUNK)),
        'gmlp_w_out': nrm(ks[13], (N_A_LAYERS, D_GMLP, D_MODEL), D_GMLP),
        'mla_w_dq': nrm(ks[14], (N_B_LAYERS, D_MODEL, Q_LORA), D_MODEL),
        'mla_q_norm': gain(ks[15], (N_B_LAYERS, Q_LORA)),
        'mla_w_uq': nrm(ks[16], (N_B_LAYERS, Q_LORA, N_HEADS, QK_DIM), Q_LORA),
        'mla_w_dkv': nrm(ks[17], (N_B_LAYERS, D_MODEL, KV_LORA + ROPE_DIM), D_MODEL),
        'mla_kv_norm': gain(ks[18], (N_B_LAYERS, KV_LORA)),
        'mla_w_uk': nrm(ks[19], (N_B_LAYERS, KV_LORA, N_HEADS, NOPE_DIM), KV_LORA),
        'mla_w_uv': nrm(ks[20], (N_B_LAYERS, KV_LORA, N_HEADS, V_DIM), KV_LORA),
        'mla_qk_gain_q': gain(ks[21], (N_B_LAYERS, QK_DIM)),
        'mla_qk_gain_k': gain(ks[22], (N_B_LAYERS, QK_DIM)),
        'mla_w_o': nrm(ks[23], (N_B_LAYERS, N_HEADS * V_DIM, D_MODEL), N_HEADS * V_DIM),
    }

def reference(x_prompt, x_sample, cache_mla, page_table, norm_g, ffn_w_gate, ffn_w_up, ffn_w_down,
              gmlp_w_in, gmlp_b_in, gmlp_v_norm, gmlp_w_s, gmlp_b_s, gmlp_w_out,
              mla_w_dq, mla_q_norm, mla_w_uq, mla_w_dkv, mla_kv_norm, mla_w_uk, mla_w_uv,
              mla_qk_gain_q, mla_qk_gain_k, mla_w_o):
    s_prompt = x_prompt.shape[1]
    n_dec, s_dec = x_sample.shape[0], x_sample.shape[1]
    past_len = page_table.shape[1] * cache_mla.shape[2]
    pos_p = jnp.arange(s_prompt, dtype=jnp.int32)
    pos_s = past_len + jnp.arange(s_dec, dtype=jnp.int32)
    kpos_s = jnp.arange(past_len + s_dec, dtype=jnp.int32)

    def half_ffn(x, i, k):
        h = rms_norm(x, norm_g[i, 2 * k])
        return x + 0.5 * swiglu(h, ffn_w_gate[i, k], ffn_w_up[i, k], ffn_w_down[i, k])

    xp, xs = x_prompt, x_sample
    new_mla_p, new_mla_s, new_v_s = [], [], []
    for i in range(DEPTH):
        xp = half_ffn(xp, i, 0)
        xs = half_ffn(xs, i, 0)
        hp = rms_norm(xp, norm_g[i, 1])
        hs = rms_norm(xs, norm_g[i, 1])
        j = i // N_MIXERS
        if i % N_MIXERS == 0:
            a_args = (gmlp_w_in[j], gmlp_b_in[j], gmlp_v_norm[j], gmlp_w_s[j], gmlp_b_s[j], gmlp_w_out[j])
            yp, _ = gmlp_mixer(hp, *a_args)
            ys, v_s = gmlp_mixer(hs, *a_args)
            new_v_s.append(v_s)
        else:
            p_args = (mla_w_dq[j], mla_q_norm[j], mla_w_uq[j], mla_w_dkv[j], mla_kv_norm[j],
                      mla_w_uk[j], mla_qk_gain_q[j], mla_qk_gain_k[j])
            ql_p, qr_p, rows_p = mla_project(hp, pos_p, *p_args)
            yp = mla_attend(ql_p, qr_p, pos_p, rows_p, pos_p, mla_w_uv[j], mla_w_o[j])
            ql_s, qr_s, rows_s = mla_project(hs, pos_s, *p_args)
            past = cache_mla[j][page_table].reshape(n_dec, past_len, CACHE_DIM)
            keys_s = jnp.concatenate([past, rows_s], axis=1)
            ys = mla_attend(ql_s, qr_s, pos_s, keys_s, kpos_s, mla_w_uv[j], mla_w_o[j])
            new_mla_p.append(rows_p)
            new_mla_s.append(rows_s)
        xp = xp + yp
        xs = xs + ys
        xp = half_ffn(xp, i, 1)
        xs = half_ffn(xs, i, 1)

    new_mla_prompt = jnp.stack(new_mla_p)
    new_mla_sample = jnp.stack(new_mla_s)
    new_gmlp_v_sample = jnp.stack(new_v_s)
    return (xp, xs, new_mla_prompt, new_mla_sample, new_gmlp_v_sample)


_drawn_inputs = setup_inputs


def setup_inputs(seed=0):
    import zlib

    import numpy as np

    out = dict(_drawn_inputs(seed))
    spreads = {}
    factors = {'gmlp_b_in': 2.696, 'mla_q_norm': 5.705, 'mla_qk_gain_q': 5.202, 'mla_qk_gain_k': 5.852}
    for name, (base, spread) in spreads.items():
        noise = np.random.default_rng([zlib.crc32(name.encode()), seed]).standard_normal(out[name].shape)
        drawn = base * np.exp(spread * noise) if base else spread * noise
        out[name] = jnp.asarray(drawn.astype(out[name].dtype))
    for name, factor in factors.items():
        out[name] = (out[name] * factor).astype(out[name].dtype)
    return out
```

```python
from contextlib import ExitStack

import numpy as np

import concourse.bass as bass
from concourse import mybir

P = 128
F32, F32R, I32 = mybir.dt.float32, mybir.dt.float32r, mybir.dt.int32
ALU, ACT, AX = mybir.AluOpType, mybir.ActivationFunctionType, mybir.AxisListType

SEQ, NS = 512, 8
TOK = SEQ + NS
HALF = TOK // 2
QB = SEQ // P
D = 1024
KD = D // P
FF = 2816
FF_GROUPS = (4, 4, 3)
GM = 2048
GT = GM // P
NG = 8
H, QL, KL, NOPE, ROPE, VD = 16, 256, 128, 128, 64, 128
QK = NOPE + ROPE
CD = KL + ROPE + H
PAST, PAGE = 1024, 128
NP = PAST // PAGE
POOL = 80
THETA = 10000.0
EPS = 1e-6
NEG = -1e30
KC = 8
WC = 256
SLOT = KC * WC


def constants():
    ident = np.eye(P, dtype=np.float32)
    ones = np.ones((P, P), np.float32)
    r = np.arange(P)
    swap = np.zeros((P, P), np.float32)
    swap[r, r ^ (ROPE // 2)] = 1.0
    causal = np.where(r[None, :] > r[:, None], np.float32(NEG), np.float32(0.0))
    own = np.where(r[:, None] // H == np.arange(NS)[None, :], np.float32(0.0), np.float32(NEG))
    own_rows = np.zeros((P, P), np.float32)
    own_rows[:NS] = (np.arange(NS)[:, None] == r[None, :] // H)
    two = (r[:, None] // ROPE == np.arange(2)[None, :]).astype(np.float32)
    half = ROPE // 2
    inv = np.float32(THETA) ** (-np.arange(half, dtype=np.float32) / np.float32(half))
    pos = np.concatenate([np.arange(SEQ), np.full(NS, PAST)]).astype(np.float32)
    ang = inv[r % half][:, None] * pos[None, :]
    cos = np.cos(ang).astype(np.float32)
    sin = np.sin(ang).astype(np.float32) * np.where(r % ROPE < half, -1.0, 1.0).astype(np.float32)[:, None]
    return np.concatenate([ident, ones, swap, causal, own, own_rows, two, cos, sin], axis=1).astype(np.float32)


N_CONST = 4 * P + NS + P + 2
N_TRIG = 2 * TOK


class At:

    FIELDS = ("chunk", "tile", "evac", "h", "mul", "act", "norm", "rms", "sums")

    def __init__(self, **counts):
        self.chunk, self.tile, self.evac, self.h, self.mul, self.act, self.norm, self.rms, self.sums = (
            counts.get(f, 0) for f in self.FIELDS)

    def past(self, chunk=0, tile=0, evac=0, h=0, mul=0, act=0, norm=0, rms=0, sums=0):
        return At(chunk=self.chunk + chunk, tile=self.tile + tile, evac=self.evac + evac, h=self.h + h,
                  mul=self.mul + mul, act=self.act + act, norm=self.norm + norm, rms=self.rms + rms, sums=self.sums + sums)


def ffn_past(at, last=False):
    pairs = sum(FF_GROUPS)
    chunks = 2 * pairs + 4 * len(FF_GROUPS)
    return at.past(chunks, 2 * chunks, 2 * chunks, 2 * pairs, 2 * pairs, 2 * pairs, 1, 1, 0 if last else KD)


def bc(ap, n):
    return ap.unsqueeze(len(ap.shape)).to_broadcast(list(ap.shape) + [n])


def halves(ap):
    return ap.rearrange("p (h n) -> p h n", h=2)


def program(nc, x_prompt, x_sample, cache_mla, page_table, norm_g, ffn_w_gate, ffn_w_up, ffn_w_down,
            gmlp_w_in, gmlp_b_in, gmlp_v_norm, gmlp_w_s, gmlp_b_s, gmlp_w_out,
            mla_w_dq, mla_q_norm, mla_w_uq, mla_w_dkv, mla_kv_norm, mla_w_uk, mla_w_uv,
            mla_qk_gain_q, mla_qk_gain_k, mla_w_o,
            y_prompt, y_sample, new_prompt, new_sample, new_v):
    table = nc.inline_tensor(constants(), name="shape_constants").ap()

    with ExitStack() as ctx:
        def sb(name, shape, dt=F32, at=ctx):
            return at.enter_context(nc.sbuf_tensor(name, shape, dt))

        def sem(name):
            return ctx.enter_context(nc.semaphore(name))

        x = sb("x", [P, KD, TOK])
        h_hi = sb("h_hi", [P, KC, TOK], F32R)
        h_lo = sb("h_lo", [P, KC, TOK], F32R)
        raw = sb("raw", [P, 2, SLOT])
        w_hi = sb("w_hi", [P, 2, SLOT], F32R)
        w_lo = sb("w_lo", [P, 2, SLOT], F32R)
        rstd_all = sb("rstd_all", [P, TOK])
        square = sb("square", [P, 2, TOK])
        square_sum = sb("square_sum", [P, TOK])
        root = sb("root", [P, TOK])
        const = sb("const", [P, N_CONST])
        eps = sb("eps", [P, 1])
        vectors = sb("vectors", [P, P])
        ident, ones, swap, causal = (const[:, i * P:(i + 1) * P] for i in range(4))
        own = const[:, 4 * P:4 * P + NS]
        own_rows = const[0:NS, 4 * P + NS:5 * P + NS]
        two = const[:, 5 * P + NS:5 * P + NS + 2]
        n_gain, n_bias, n_vg = 6 * KD, 2 * GT, GT
        gain = vectors[:, 0:n_gain].rearrange("p (n k) -> p n k", k=KD)
        b_in = vectors[:, n_gain:n_gain + n_bias]
        v_gain = vectors[:, n_gain + n_bias:n_gain + n_bias + n_vg]
        c0 = n_gain + n_bias + n_vg
        q_gain, kv_gain = vectors[:, c0:c0 + 2], vectors[:, c0 + 2:c0 + 3]
        nope_gains, rope_gains = vectors[:, c0 + 3:c0 + 5], vectors[:, c0 + 5:c0 + 7]
        n_vec = c0 + 7

        early = ExitStack()
        xg_hi = sb("xg_hi", [P, KD, TOK], F32R, early)
        xg_lo = sb("xg_lo", [P, KD, TOK], F32R, early)
        wide = ExitStack()
        v = sb("v", [P, GT, TOK], F32, wide)
        tmp_in = sb("tmp_in", [P, 2, TOK], F32, wide)
        tmp_act = sb("tmp_act", [P, 2, TOK], F32, wide)
        tmp_mul = sb("tmp_mul", [P, 2, TOK], F32, wide)
        tmp_h = sb("tmp_h", [P, 2, TOK], F32, wide)
        ws_t = sb("ws_t", [P, NG, P], F32, wide)
        bs_all = sb("bs_all", [P, NG, P], F32, wide)
        v_tok = sb("v_tok", [P, 2, QB, P], F32, wide)
        vs_tok = sb("vs_tok", [NS, 2, 2, P], F32, wide)
        ws_first = sb("ws_first", [P, NG], F32, wide)
        bs_first = sb("bs_first", [P, NG], F32, wide)
        rv_root = sb("rv_root", [P, QB + 1 + NS], F32, wide)
        rv = sb("rv", [P, QB + 1 + NS], F32, wide)
        x_tok = v[:, 0:8, :].rearrange("p a n -> p (a n)")[:, 0:QB * D].rearrange("p (q d) -> p q d", q=QB)
        xs_tok = v[0:NS, 8:10, :].rearrange("p a n -> p (a n)")[:, 0:D]
        vector_rows = v[:, 12, 0:P]
        ws_nat = v_tok[:, :, :, :].rearrange("p a q d -> p (a q) d")
        wide.close()
        early.close()

        late = ExitStack()
        qn = sb("qn", [P, H, TOK], F32, late)
        qr = sb("qr", [P, H // 2, TOK], F32, late)
        wkv = sb("wkv", [P, H, P], F32, late)
        c_t = sb("c_t", [P, TOK], F32, late)
        kr_t = sb("kr_t", [P, TOK], F32, late)
        rows = sb("rows", [P, QB, CD], F32, late)
        rows_s = sb("rows_s", [NS, CD], F32, late)
        kr_tok = sb("kr_tok", [P, QB, P], F32, late)
        ssq = sb("ssq", [P, 5 * H], F32, late)
        rq = sb("rq", [P, 5 * H], F32, late)
        ks = sb("ks", [P, 5 * H], F32, late)
        krq = sb("krq", [P, 5], F32, late)
        gg = sb("gg", [P, 2], F32, late)
        o_s = sb("o_s", [P, P], F32, late)
        pages = sb("pages", [1, NS * NP], I32, late)
        few = sb("few", [P, 24], F32, late)
        krq_s = sb("krq_s", [P, NS], F32, late)[:, :]
        inv_sum = sb("inv_sum", [P, QB], F32, late)[:, :]
        proj = ExitStack()
        trig = sb("trig", [P, 2, TOK], F32, proj)
        cq = sb("cq", [P, 2, TOK], F32, proj)
        trig_g = sb("trig_g", [P, 2, TOK], F32, proj)
        tq = sb("tq", [P, 2, TOK], F32, proj)
        rope_a = sb("rope_a", [P, TOK], F32, proj)
        rope_b = sb("rope_b", [P, TOK], F32, proj)
        sq_h = sb("sq_h", [P, 2, TOK], F32, proj)
        kr_raw = rope_a[:, :]
        wuk_t = sb("wuk_t", [P, 2, P], F32, proj)
        proj.close()
        dec = ExitStack()
        nat = sb("nat", [P, 2, 4, CD], F32, dec)
        kr_dup = sb("kr_dup", [P, 2, 4, P], F32, dec)
        kt = sb("kt", [P, 2, 2, 512], F32, dec)
        q_pad = sb("q_pad", [P, 2, NS, P], F32, dec)
        q_all = sb("q_all", [P, 2, P], F32, dec)
        sd = kt[:, :, :, :].rearrange("p a b c -> p (a b c)")[:, 0:PAST + NS]
        ks_all = square[:, :, :].rearrange("p a n -> p (a n)")[:, 0:NP * P].rearrange("p (j c) -> p j c", j=NP)
        ks_new = square_sum[0:NS, 0:2 * P].rearrange("p (a c) -> p a c", a=2)
        p_new = square_sum[0:NS, 2 * P:3 * P]
        dec.close()
        heads = ExitStack()
        diag = sb("diag", [P, QB, P], F32, heads)
        cks = sb("cks", [P, 2, SEQ], F32, heads)
        krs = sb("krs", [P, 2, SEQ], F32, heads)
        prob = sb("prob", [P, 2, 10 * P], F32, heads)
        prob_t = sb("prob_t", [P, 10 * P], F32, heads)
        o_t = sb("o_t", [P, TOK], F32, heads)
        heads.close()
        late.close()

        main = ctx.enter_context(nc.psum_tensor("main", [P, 2, 2, 512], F32))
        side = ctx.enter_context(nc.psum_tensor("side", [P, 4, 512], F32))

        const_in = sem("const_in")
        vectors_in = sem("vectors_in")
        vectors_turned = sem("vectors_turned")
        vectors_set = sem("vectors_set")
        ws_in = sem("ws_in")
        raw_in = [sem("raw_in0"), sem("raw_in1")]
        hi_done = sem("hi_done")
        lo_done = sem("lo_done")
        tile_done = sem("tile_done")
        evac_done = sem("evac_done")
        act_done = sem("act_done")
        mul_done = sem("mul_done")
        h_hi_done = sem("h_hi_done")
        h_lo_done = sem("h_lo_done")
        xg_hi_done = sem("xg_hi_done")
        xg_lo_done = sem("xg_lo_done")
        square_done = sem("square_done")
        sum_done = sem("sum_done")
        rms_mm = sem("rms_mm")
        root_done = sem("root_done")
        rstd_done = sem("rstd_done")
        eps_set = sem("eps_set")
        out_turned = sem("out_turned")
        out_copied = sem("out_copied")
        out_written = sem("out_written")
        ws_masked = sem("ws_masked")
        ws_turned = sem("ws_turned")
        ws_copied = sem("ws_copied")
        vg_done = sem("vg_done")
        v_turned = sem("v_turned")
        v_copied = sem("v_copied")
        vs_out = [sem("vs_out0"), sem("vs_out1")]
        mix_done = sem("mix_done")
        mixed = sem("mixed")
        v_seen = sem("v_seen")
        sample_mix = sem("sample_mix")

        kv_in = sem("kv_in")
        pages_in = sem("pages_in")
        nat_in0 = sem("nat_in0")
        nat_in1 = sem("nat_in1")
        gg_set = sem("gg_set")
        trig_set = sem("trig_set")
        cq_squared = sem("cq_squared")
        cqn_set = sem("cqn_set")
        c_squared = sem("c_squared")
        c_set = sem("c_set")
        kr_swapped = sem("kr_swapped")
        kr_part = sem("kr_part")
        kr_set = sem("kr_set")
        rope_part = sem("rope_part")
        row_turned = sem("row_turned")
        row_copied = sem("row_copied")
        rows_done = sem("rows_done")
        tq_read = sem("tq_read")
        q_ssq = sem("q_ssq")
        swapped = sem("swapped")
        rope_b_set = sem("rope_b_set")
        rope_a_set = sem("rope_a_set")
        qr_set = sem("qr_set")
        q_ssq_read = sem("q_ssq_read")
        wuk_turned = sem("wuk_turned")
        wuk_copied = sem("wuk_copied")
        kn_done = sem("kn_done")
        kn_squared = sem("kn_squared")
        k_ssq = sem("k_ssq")
        lat_done = sem("lat_done")
        lat_copied = sem("lat_copied")
        kr_squared = sem("kr_squared")
        ssq_set = sem("ssq_set")
        ssq_root = sem("ssq_root")
        scale_set = sem("scale_set")
        qpad_zero = sem("qpad_zero")
        q_all_set = sem("q_all_set")
        q_pad_set = sem("q_pad_set")
        nat_dup = sem("nat_dup")
        nat_turned = sem("nat_turned")
        kt_c_copied = sem("kt_c_copied")
        kt_r_copied = sem("kt_r_copied")
        nat_used = sem("nat_used")
        ks_turned = sem("ks_turned")
        ks_copied = sem("ks_copied")
        new_scored = sem("new_scored")
        ks_new_set = sem("ks_new_set")
        new_ready = sem("new_ready")
        sd_set = sem("sd_set")
        sd_max = sem("sd_max")
        sd_exp = sem("sd_exp")
        sd_inv = sem("sd_inv")
        sd_prob = sem("sd_prob")
        sd_turned = sem("sd_turned")
        sd_t_copied = sem("sd_t_copied")
        pv_used = sem("pv_used")
        os_done = sem("os_done")
        os_copied = sem("os_copied")
        diag_set = sem("diag_set")
        k_scaled = sem("k_scaled")
        cks_copied = sem("cks_copied")
        krs_copied = sem("krs_copied")
        scored = sem("scored")
        max_set = sem("max_set")
        max_done = sem("max_done")
        exp_done = sem("exp_done")
        inv_done = sem("inv_done")
        prob_done = sem("prob_done")
        prob_turned = sem("prob_turned")
        prob_t_act = sem("prob_t_act")
        prob_t_dve = sem("prob_t_dve")
        pv_done = sem("pv_done")
        o_copied = sem("o_copied")
        o_samples = sem("o_samples")
        uv_done = sem("uv_done")
        uv_copied = sem("uv_copied")
        tq_squared = sem("tq_squared")
        dkv_rope_in = sem("dkv_rope_in")
        uq_rope_in = [sem("uq_rope_in0"), sem("uq_rope_in1")]
        nat_in = [nat_in0, nat_in1]

        at_ffn = [None] * 4
        at_ffn[0] = At(tile=KD, evac=KD, sums=KD)
        at_gmlp = ffn_past(at_ffn[0])
        n_v, n_u, n_out = GT // 2, GT // 2, 8
        gmlp_chunks = n_v + n_u + n_out
        at_ffn[1] = at_gmlp.past(gmlp_chunks, 2 * gmlp_chunks, 2 * gmlp_chunks, GT, GT, 2 * GT, 1, 2, GT + KD)
        at_ffn[2] = ffn_past(at_ffn[1])
        at_mla = ffn_past(at_ffn[2])
        at_uq = at_mla.past(chunk=2, tile=4, evac=4, h=2, rms=3)
        at_wo = at_uq.past(chunk=4, tile=24, evac=24)
        at_ffn[3] = at_wo.past(chunk=8, tile=16, evac=16, h=H, norm=1, sums=KD)
        P_AT = [0, 1, 3, 6]
        PT_AT = [0, 4, 7, 9]
        at_end = ffn_past(at_ffn[3], last=True)
        last_chunk = at_end.chunk - 1
        norm_of = [(0, 0), (0, 1), (0, 2), (1, 0), (1, 1), (1, 2)]

        def w_rows(w):
            return w.rearrange("(k p) n -> p k n", p=P)

        block = ctx.enter_context(nc.Block())

        @block.sync
        def _(sp):
            sp.dma_start(x_tok, x_prompt[0].rearrange("(q p) d -> p q d", p=P)).then_inc(const_in, 16)
            sp.dma_start(xs_tok, x_sample[:, 0, :]).then_inc(const_in, 16)
            sp.dma_start(const[:], table[:, 0:N_CONST]).then_inc(const_in, 16)
            row0 = 0
            for src, n in ((norm_g.rearrange("i j (k p) -> (i j k) p", p=P), n_gain),
                           (gmlp_b_in[0].rearrange("(k p) -> k p", p=P), n_bias),
                           (gmlp_v_norm[0].rearrange("(k p) -> k p", p=P), n_vg),
                           (mla_q_norm[0].rearrange("(k p) -> k p", p=P), 2), (mla_kv_norm, 1),
                           (mla_qk_gain_q[:, 0:NOPE], 1), (mla_qk_gain_k[:, 0:NOPE], 1)):
                sp.dma_start(vector_rows[row0:row0 + n, :], src).then_inc(vectors_in, 16)
                row0 += n
            for src in (mla_qk_gain_q, mla_qk_gain_k):
                for a in range(2):
                    sp.dma_start(vector_rows[row0:row0 + 1, a * ROPE:(a + 1) * ROPE],
                                 src[:, NOPE:QK]).then_inc(vectors_in, 16)
                row0 += 1

            def load(n, slot, w, k0, nk, c0, nc_=WC):
                if not isinstance(n, int) or n >= 2:
                    sp.wait_ge(lo_done, n - 1)
                dst = raw[:, slot, :].rearrange("p (k c) -> p k c", k=KC)[:, 0:nk, 0:nc_]
                cols = slice(c0, c0 + nc_) if isinstance(c0, int) else bass.ds(c0, nc_)
                sp.dma_start(dst, w_rows(w)[:, k0:k0 + nk, cols]).then_inc(raw_in[slot], 16)

            def ffn(at, layer, which):
                wg, wu, wd = ffn_w_gate[layer, which], ffn_w_up[layer, which], ffn_w_down[layer, which]
                n, f0 = at.chunk, 0
                for pairs in FF_GROUPS:
                    def gate_up(i, n=n, f0=f0):
                        load(n + 2 * i, 0, wg, 0, KD, (f0 + i) * WC)
                        load(n + 2 * i + 1, 1, wu, 0, KD, (f0 + i) * WC)
                    start = 1 if n < 2 else 0
                    if start:
                        gate_up(0)
                    with sp.Fori(0, pairs - start) as i:
                        gate_up(i + start)
                    n += 2 * pairs

                    with sp.Fori(0, 2) as i:
                        for s in range(2):
                            load(n + 2 * i + s, s, wd, 2 * f0, 2 * pairs, (2 * i + s) * WC)
                    n += 4
                    f0 += pairs

            ffn(at_ffn[0], 0, 0)
            n = at_gmlp.chunk
            with sp.Fori(0, n_v // 2) as i:
                for s in range(2):
                    load(n + 2 * i + s, s, gmlp_w_in[0], 0, KD, (2 * i + s) * WC + GM)
            n += n_v
            for q in range(2):
                with sp.Fori(0, n_u // 4) as i:
                    for s in range(2):
                        load(n + 2 * i + s, s, gmlp_w_in[0], 0, KD, (2 * i + s) * WC + q * GM // 2)
                n += n_u // 2
                with sp.Fori(0, 2) as i:
                    for s in range(2):
                        load(n + 2 * i + s, s, gmlp_w_out[0], q * KC, KC, (2 * i + s) * WC)
                n += 4
            ffn(at_ffn[1], 0, 1)
            ffn(at_ffn[2], 1, 0)

            n = at_mla.chunk
            load(n, 0, mla_w_dq[0], 0, KD, 0)
            sp.wait_ge(lo_done, n)
            dst = raw[:, 1, :].rearrange("p (k c) -> p k c", k=KC)
            sp.dma_start(dst[:, :, 0:KL + ROPE], w_rows(mla_w_dkv[0])).then_inc(raw_in[1], 16)
            sp.dma_start(dst[:, :, KL + ROPE:KL + 2 * ROPE], w_rows(mla_w_dkv[0])[:, :, KL:KL + ROPE]).then_inc(dkv_rope_in, 16)
            sp.dma_start(wkv[:], mla_w_uk[0]).then_inc(kv_in, 16)
            sp.wait_ge(h_lo_done, at_mla.h)
            sp.dma_start(trig[:].rearrange("p a n -> p (a n)"), table[:, N_CONST:N_CONST + N_TRIG]).then_inc(kv_in, 16)
            n = at_uq.chunk
            for c in range(4):
                sp.wait_ge(lo_done, n + c - 1)
                src = mla_w_uq[0].rearrange("(k p) h d -> k p h d", p=P)[:, :, 4 * c:4 * c + 4, :]
                for k in range(2):
                    dst = raw[:, c % 2, k * 1024:k * 1024 + 4 * QK]
                    sp.dma_start(dst[:, 4 * NOPE:].rearrange("p (h d) -> p h d", h=4), src[k, :, :, NOPE:QK])\
                        .then_inc(uq_rope_in[c % 2], 16)
                    sp.dma_start(dst[:, 0:4 * NOPE].rearrange("p (h d) -> p h d", h=4), src[k, :, :, 0:NOPE])\
                        .then_inc(uq_rope_in[c % 2] if k else raw_in[c % 2], 16)
            sp.dma_start(pages[:], page_table.rearrange("b n -> (b n)").unsqueeze(0)).then_inc(pages_in, 16)
            sp.wait_ge(rows_done, 1)
            sp.dma_start(new_prompt[0, 0].rearrange("(q p) d -> p q d", p=P), rows[:]).then_inc(out_written, 16)
            sp.dma_start(new_sample[0, :, 0, :], rows_s[:]).then_inc(out_written, 16)
            sp.wait_ge(pages_in, 16)
            sp.wait_ge(lat_done, H)
            for half in range(4 * NS):
                again = half >= 2 * NS
                k = half % (2 * NS)
                if 2 <= half < 2 * NS + 2:
                    sp.wait_ge(nat_turned, 2 * (half - 1))
                    sp.wait_ge(nat_dup, half - 1)
                elif again:
                    sp.wait_ge(pv_used, half - 2 * NS - 1)
                for j in range(4):
                    page = sp.value_load(pages[0:1, 4 * k + j:4 * k + j + 1], min_val=0, max_val=POOL - 1)
                    sp.dma_start(nat[:, half % 2, j, 0:CD],
                                 cache_mla[0, bass.ds(page, 1), :, :].rearrange("a p d -> (a p) d"))\
                        .then_inc(nat_in[half % 2], 16)
            sp.wait_ge(lat_done, H)
            sp.dma_start(wkv[:], mla_w_uv[0]).then_inc(kv_in, 16)
            n = at_wo.chunk
            for q in range(2):
                for c in range(4):
                    load(n, c % 2, mla_w_o[0], q * KC, KC, c * WC)
                    n += 1
            ffn(at_ffn[3], 1, 1)
            sp.wait_ge(out_copied, KD)
            yt = x_tok
            sp.dma_start(y_prompt[0].rearrange("(q p) d -> p q d", p=P), yt).then_inc(out_written, 16)
            sp.dma_start(y_sample[:, 0, :], xs_tok).then_inc(out_written, 16)
            sp.wait_ge(out_written, 64)

        @block.tensor
        def _(pe):
            def out_tile(at_tile, m, slot, k_tiles, hi, lo, cols=None, width=P, before=None, free=None, first=True, last=True):
                if free is not None:
                    pe.wait_ge(evac_done, free)
                ws = [w[:, slot, :].rearrange("p (k c) -> p k c", k=KC) for w in (w_hi, w_lo)]
                for k in range(k_tiles):
                    if before and k in before:
                        before[k]()
                    for n, (w, moving) in enumerate(((ws[0], hi), (ws[0], lo), (ws[1], hi))):
                        for half in range(2):
                            mm = nc.tensor.matmul(main[0:width, m, half, 0:HALF], w[:, k, m * P:m * P + width],
                                                  moving[:, k, half * HALF:(half + 1) * HALF],
                                                  start=(k == 0 and n == 0), stop=(k == k_tiles - 1 and n == 2))
                mm.then_inc(tile_done, 1)

            def rms(at):
                def go():
                    pe.wait_ge(sum_done, at.sums)
                    for half in range(2):
                        mm = nc.tensor.matmul(side[:, half, 0:HALF], ones, square_sum[:, half * HALF:(half + 1) * HALF],
                                              start=True, stop=True)
                    mm.then_inc(rms_mm, 1)
                return go

            def down(n, e, h, k_tiles, m_tiles=2, slot=0):
                pe.wait_ge(lo_done, n + 1)
                for m in range(2):
                    before = {}
                    if m == 0:
                        pe.wait_ge(h_lo_done, h + k_tiles - 2)
                        before[k_tiles - 2] = lambda: pe.wait_ge(h_lo_done, h + k_tiles)
                    out_tile(None, m, slot, k_tiles, h_hi, h_lo, before=before, free=e + m - 1)

            def ffn(at, final):
                n, e, h = at.chunk, at.evac, at.h
                for g, pairs in enumerate(FF_GROUPS):
                    def gate_up(i, n=n, e=e, rms_at=None):
                        for s in range(2):
                            pe.wait_ge(lo_done, n + 2 * i + s + 1)
                            for m in range(2):
                                before = {4: rms_at} if rms_at and s == 0 and m == 0 else {}
                                if rms_at and s == 0 and m == 0:
                                    pe.wait_ge(xg_lo_done, KD * at.norm + KD - 2)
                                    before[KD - 2] = lambda: pe.wait_ge(xg_lo_done, KD * at.norm + KD)
                                out_tile(None, m, s, KD, xg_hi, xg_lo, before=before, free=e + 4 * i + 2 * s + m - 1)
                    start = 0
                    if g == 0:
                        gate_up(0, rms_at=rms(at))
                        start = 1
                    with pe.Fori(0, pairs - start) as i:
                        gate_up(i + start)
                    n, e, h = n + 2 * pairs, e + 4 * pairs, h + 2 * pairs
                    if g + 1 < len(FF_GROUPS):
                        with pe.Fori(0, 2) as i:
                            for s in range(2):
                                down(n + 2 * i + s, e + 4 * i + 2 * s, h - 2 * pairs, 2 * pairs, slot=s)
                    else:
                        for i in range(4):
                            down(n + i, e + 2 * i, h - 2 * pairs, 2 * pairs, slot=i % 2)
                    n, e = n + 4, e + 8

            pe.wait_ge(const_in, 16 * 3)
            pe.wait_ge(vectors_in, 16 * 11)
            nc.tensor.transpose(side[:, 0, 0:n_vec], vector_rows[0:n_vec, :], ident[0:n_vec, 0:n_vec]).then_inc(vectors_turned, 1)
            for k in range(KD):
                if k >= 2:
                    pe.wait_ge(evac_done, k - 1)
                for q in range(QB):
                    nc.tensor.transpose(main[:, k % 2, 0, q * P:(q + 1) * P], x_tok[:, q, k * P:(k + 1) * P], ident)
                nc.tensor.transpose(main[:, k % 2, 1, 0:NS], xs_tok[:, k * P:(k + 1) * P],
                                    ident[0:NS, 0:NS]).then_inc(tile_done, 1)
            pe.wait_ge(ws_masked, 1)
            for g in range(NG):
                if g >= 2:
                    pe.wait_ge(ws_copied, g - 1)
                nc.tensor.transpose(side[:, 2 + g % 2, 0:P], ws_nat[:, g, :], ident).then_inc(ws_turned, 1)
            ffn(at_ffn[0], False)

            n, e = at_gmlp.chunk, at_gmlp.evac

            def v_chunk(i, s, first=False):
                pe.wait_ge(lo_done, n + 2 * i + s + 1)
                for m in range(2):
                    before = {}
                    if first and m == 0:
                        pe.wait_ge(xg_lo_done, KD * at_gmlp.norm + KD - 2)
                        before = {4: rms(at_gmlp), KD - 2: lambda: pe.wait_ge(xg_lo_done, KD * at_gmlp.norm + KD)}
                    out_tile(None, m, s, KD, xg_hi, xg_lo, before=before, free=e + 4 * i + 2 * s + m - 1)
            v_chunk(0, 0, True)
            v_chunk(0, 1)
            with pe.Fori(0, n_v // 2 - 1) as i:
                v_chunk(i + 1, 0)
                v_chunk(i + 1, 1)
            n, e = n + n_v, e + 2 * n_v

            def rms_v():
                pe.wait_ge(sum_done, at_gmlp.sums + GT)
                for q in range(QB):
                    nc.tensor.matmul(side[:, 2, q:q + 1], square_sum[:, q * P:(q + 1) * P], ones[:, 0:1],
                                     start=True, stop=True)
                nc.tensor.matmul(side[:, 2, QB:QB + NS], ones, square_sum[:, SEQ:TOK], start=True, stop=True)
                nc.tensor.matmul(side[0:NS, 2, QB + NS:QB + NS + 1], square_sum[:, SEQ:TOK], ones[:, 0:1],
                                 start=True, stop=True).then_inc(rms_mm, 1)

            for g in range(NG):
                if g == NG // 2:
                    for i in range(2):
                        for s in range(2):
                            down(n, e, at_gmlp.h, KC, slot=s)
                            n, e = n + 1, e + 2
                pe.wait_ge(lo_done, n + 1)
                out_tile(None, 0, g % 2, KD, xg_hi, xg_lo, before={4: rms_v} if g == 0 else {}, free=e - 1)
                pe.wait_ge(vg_done, 2 * g + 2)
                if g == 0:
                    pe.wait_ge(root_done, at_gmlp.rms + 2)
                else:
                    pe.wait_ge(mixed, 2 * g)
                    pe.wait_ge(v_seen, g)
                for m in range(2):
                    for q in range(QB):
                        nc.tensor.transpose(side[:, m, q * P:(q + 1) * P], v[:, 2 * g + m, q * P:(q + 1) * P], ident)
                    t = nc.tensor.transpose(side[0:NS, 2, m * P:(m + 1) * P], v[:, 2 * g + m, SEQ:TOK], ident)
                t.then_inc(v_turned, 1)
                out_tile(None, 1, g % 2, KD, xg_hi, xg_lo, free=e)
                for m in range(2):
                    pe.wait_ge(v_copied, 2 * g + m + 1)
                    pe.wait_ge(ws_copied, NG)
                    bank = (3, 0)[m]
                    for q in range(QB):
                        mm = nc.tensor.matmul(side[:, bank, q * P:(q + 1) * P], v_tok[:, m, q, :], ws_t[:, g, :],
                                              start=True, stop=True)
                    mm.then_inc(mix_done, 1)
                n, e = n + 1, e + 2
            for i in range(4):
                down(n, e, at_gmlp.h + KC, KC, slot=i % 2)
                n, e = n + 1, e + 2
            ffn(at_ffn[1], False)
            ffn(at_ffn[2], False)

            n, e = at_mla.chunk, at_mla.evac
            pe.wait_ge(xg_lo_done, KD * at_mla.norm + KD - 2)
            pe.wait_ge(lo_done, n + 1)
            out_tile(None, 0, 0, KD, xg_hi, xg_lo, free=e - 1,
                     before={4: rms(at_mla), KD - 2: lambda: pe.wait_ge(xg_lo_done, KD * at_mla.norm + KD)})
            out_tile(None, 1, 0, KD, xg_hi, xg_lo, free=e)
            pe.wait_ge(lo_done, n + 2)
            out_tile(None, 0, 1, KD, xg_hi, xg_lo, free=e + 1)

            def wide_sum(bank, stationary, moving, parts=1):
                for half in range(2):
                    for i in range(parts):
                        mm = nc.tensor.matmul(side[:, bank + half, 0:HALF], stationary,
                                              moving[i][:, half * HALF:(half + 1) * HALF],
                                              start=(i == 0), stop=(i == parts - 1))
                return mm

            pe.wait_ge(cq_squared, 2)
            pe.wait_ge(root_done, at_mla.rms + 1)
            wide_sum(0, ones, [square[:, 0, :], square[:, 1, :]], 2).then_inc(rms_mm, 1)
            out_tile(None, 1, 1, KD, xg_hi, xg_lo, free=e + 2)
            pe.wait_ge(c_squared, 1)
            wide_sum(2, ones, [tq[:, 0, :]]).then_inc(rms_mm, 1)
            pe.wait_ge(evac_done, e + 4)
            pe.wait_ge(root_done, at_mla.rms + 2)
            wide_sum(0, swap, [kr_raw]).then_inc(kr_swapped, 1)

            n, e = at_uq.chunk, at_uq.evac
            pe.wait_ge(h_lo_done, at_uq.h)

            def q_after(u):
                c, part = u // 6, u % 6
                rope = part % 3 == 2
                if rope:
                    r_ = 2 * c + part // 3
                    pe.wait_ge(rope_b_set, r_ + 1)
                    pe.wait_ge(evac_done, e + u + 1)
                    wide_sum(0, swap, [tq[:, u % 2, :]]).then_inc(swapped, 1)
                pe.wait_ge(tq_squared, u + 1)
                h0 = 4 * c + 2 * (part // 3)
                base, hh, w = (5 * H, h0, 2) if rope else (0, h0 + part % 3, 1)
                rhs = two if rope else ones[:, 0:1]
                for b in range(QB + 1):
                    rows_ = P if b < QB else NS
                    mm = nc.tensor.matmul(side[0:rows_, 2, base + b * H + hh:base + b * H + hh + w],
                                          sq_h[:, u % 2, b * P:b * P + rows_], rhs, start=True, stop=True)
                mm.then_inc(q_ssq, 1)

            pe.wait_ge(root_done, at_uq.rms)
            for u in range(24):
                c, part = u // 6, u % 6
                if part == 0:
                    pe.wait_ge(lo_done, n + c + 1)
                pe.wait_ge(evac_done, e + u - 1)
                h0 = 2 * (part // 3)
                for k in range(2):
                    for i, (w, moving) in enumerate(((w_hi, h_hi), (w_hi, h_lo), (w_lo, h_hi))):
                        col = k * 1024 + (4 * NOPE + h0 * ROPE if part % 3 == 2 else (h0 + part % 3) * NOPE)
                        st = w[:, c % 2, col:col + P]
                        for half in range(2):
                            mm = nc.tensor.matmul(main[:, u % 2, half, 0:HALF], st,
                                                  moving[:, k, half * HALF:(half + 1) * HALF],
                                                  start=(k == 0 and i == 0), stop=(k == 1 and i == 2))
                mm.then_inc(tile_done, 1)
                if u > 0:
                    q_after(u - 1)
            q_after(23)

            pe.wait_ge(rope_b_set, 9)
            pe.wait_ge(evac_done, at_wo.evac)
            for b in range(QB + 1):
                w = P if b < QB else NS
                if b == 0:
                    pe.wait_ge(c_set, 1)
                    pe.wait_ge(kr_set, 1)
                if b >= 2:
                    pe.wait_ge(row_copied, b - 1)
                nc.tensor.transpose(side[0:w, b % 2, 0:P], c_t[:, b * P:b * P + w], ident)
                nc.tensor.transpose(side[0:w, b % 2, P:2 * P], kr_t[:, b * P:b * P + w], ident).then_inc(row_turned, 1)
            pe.wait_ge(kv_in, 32)
            pe.wait_ge(kr_squared, 1)
            for b in range(QB + 1):
                w = P if b < QB else NS
                nc.tensor.matmul(side[0:w, 3, 5 * H + b:5 * H + b + 1], sq_h[0:ROPE, 0, b * P:b * P + w],
                                 ones[0:ROPE, 0:1], start=True, stop=True)

            def k_norms(h):
                pe.wait_ge(kn_squared, h + 1)
                for b in range(QB + 1):
                    w = P if b < QB else NS
                    mm = nc.tensor.matmul(side[0:w, 3, b * H + h:b * H + h + 1], sq_h[:, h % 2, b * P:b * P + w],
                                          ones[:, 0:1], start=True, stop=True)
                mm.then_inc(k_ssq, 1)

            for h in range(H):
                if h == 0:
                    pe.wait_ge(row_copied, QB + 1)
                if h >= 2:
                    pe.wait_ge(wuk_copied, h - 1)
                nc.tensor.transpose(side[:, h % 2, 0:P], wkv[:, h, :], ident).then_inc(wuk_turned, 1)
                if h >= 1:
                    pe.wait_ge(kn_squared, h)
                for half in range(2):
                    mm = nc.tensor.matmul(main[:, 0, half, 0:HALF], wkv[:, h, :], c_t[:, half * HALF:(half + 1) * HALF],
                                          start=True, stop=True)
                mm.then_inc(kn_done, 1)
                if h >= 1:
                    k_norms(h - 1)
                    pe.wait_ge(lat_copied, h)
                pe.wait_ge(wuk_copied, h + 1)
                pe.wait_ge(tq_read, 24)
                for half in range(2):
                    mm = nc.tensor.matmul(main[:, 1, half, 0:HALF], wuk_t[:, h % 2, :],
                                          qn[:, h, half * HALF:(half + 1) * HALF], start=True, stop=True)
                mm.then_inc(lat_done, 1)
            k_norms(H - 1)

            pe.wait_ge(q_pad_set, 1)
            pe.wait_ge(q_ssq_read, 1)
            pe.wait_ge(ssq_set, 2)

            def turn_keys(k):
                pe.wait_ge(nat_in[k % 2], 64 * (k // 2 + 1))
                pe.wait_ge(nat_dup, k + 1)
                if k >= 2:
                    pe.wait_ge(kt_c_copied, k - 1)
                    pe.wait_ge(kt_r_copied, k - 1)
                for j in range(4):
                    t = nc.tensor.transpose(side[:, 2 * (k % 2), j * P:(j + 1) * P], nat[:, k % 2, j, 0:KL], ident)
                t.then_inc(nat_turned, 1)
                for j in range(4):
                    t = nc.tensor.transpose(side[:, 2 * (k % 2) + 1, j * P:(j + 1) * P],
                                            kr_dup[:, k % 2, j, :], ident)
                t.then_inc(nat_turned, 1)

            turn_keys(0)
            for k in range(2 * NS):
                if k + 1 < 2 * NS:
                    turn_keys(k + 1)
                b = k // 2
                pe.wait_ge(kt_c_copied, k + 1)
                nc.tensor.matmul(main[:, 0, k % 2, :], q_pad[:, 0, b, :], kt[:, k % 2, 0, :], start=(b == 0), stop=False)
                pe.wait_ge(kt_r_copied, k + 1)
                nc.tensor.matmul(main[:, 0, k % 2, :], q_pad[:, 1, b, :], kt[:, k % 2, 1, :], start=False,
                                 stop=(b == NS - 1)).then_inc(nat_used, 1)
            for j in range(NP):
                t = nc.tensor.transpose(main[:, 1, j // 4, (j % 4) * P:(j % 4 + 1) * P], ks_all[:, j, :], ident)
            t.then_inc(ks_turned, 1)
            pe.wait_ge(kt_c_copied, 2 * NS)
            pe.wait_ge(kt_r_copied, 2 * NS)
            nc.tensor.matmul(side[:, 0, 0:NS], q_all[:, 0, :], c_t[:, SEQ:TOK], start=True, stop=False)
            nc.tensor.matmul(side[:, 0, 0:NS], q_all[:, 1, :], kr_t[:, SEQ:TOK], start=False, stop=True)
            pe.wait_ge(ks_new_set, 2)
            nc.tensor.matmul(side[:, 1, 0:NS], ks_new[:, 0, :], ident[0:NS, 0:NS], start=True, stop=True)
            nc.tensor.matmul(side[:, 2, 0:1], ks_new[:, 1, :], ones[0:NS, 0:1], start=True, stop=True).then_inc(new_scored, 1)
            pe.wait_ge(sd_prob, 1)
            for j in range(NP):
                nc.tensor.transpose(main[:, 1, j // 4, (j % 4) * P:(j % 4 + 1) * P], sd[:, j * P:(j + 1) * P], ident)
            nc.tensor.transpose(side[0:NS, 3, 0:P], sd[:, PAST:PAST + NS], ident).then_inc(sd_turned, 1)
            pe.wait_ge(sd_t_copied, 2)
            for k in range(2 * NS):
                b = k // 2
                pe.wait_ge(nat_in[k % 2], 64 * (k // 2 + 1 + NS))
                for j in range(4):
                    blk = 4 * (k % 2) + j
                    mm = nc.tensor.matmul(main[:, 0, 0, b * H:(b + 1) * H], nat[:, k % 2, j, 0:KL],
                                          ks_all[:, blk, b * H:(b + 1) * H], start=(blk == 0), stop=False)
                mm.then_inc(pv_used, 1)
                if k % 2 == 1:
                    mm = nc.tensor.matmul(main[:, 0, 0, b * H:(b + 1) * H], rows_s[:, 0:KL], p_new[:, b * H:(b + 1) * H],
                                          start=False, stop=True)
            mm.then_inc(os_done, 1)

            pe.wait_ge(os_copied, 1)
            pe.wait_ge(kv_in, 48)

            def scale_keys(h):
                pe.wait_ge(diag_set, h + 1)
                if h >= 3:
                    pe.wait_ge(uv_copied, max(h - 2, KC if h >= KC else 0))
                for j in range(QB):
                    mm = nc.tensor.matmul(side[:, 0, j * P:(j + 1) * P], rows[:, j, 0:KL], diag[:, j, :], start=True, stop=True)
                mm.then_inc(k_scaled, 1)
                for j in range(QB):
                    mm = nc.tensor.matmul(side[:, 1, j * P:(j + 1) * P], kr_tok[:, j, :], diag[:, j, :], start=True, stop=True)
                mm.then_inc(k_scaled, 1)

            def scores(h):
                pe.wait_ge(cks_copied, h + 1)
                pe.wait_ge(krs_copied, h + 1)
                if h >= 1:
                    pe.wait_ge(exp_done, h)
                lo = ROPE * (h % 2)
                for q in range(QB):
                    bank = main[:, q // 2, q % 2, :]
                    nk = (q + 1) * P
                    nc.tensor.matmul(bank[:, 0:nk], qn[:, h, q * P:(q + 1) * P], cks[:, h % 2, 0:nk], start=True, stop=False)
                    nc.tensor.matmul(bank[:, 0:nk], qr[lo:lo + ROPE, h // 2, q * P:(q + 1) * P],
                                     krs[lo:lo + ROPE, h % 2, 0:nk], start=False, stop=False)
                    mm = nc.tensor.matmul(bank[:, q * P:nk], ident, causal, start=False, stop=True)
                mm.then_inc(scored, 1)

            def values(h, next_scaled):
                pe.wait_ge(prob_done, h + 1)
                if h >= 1:
                    pe.wait_ge(o_copied, h)
                    pe.wait_ge(uv_copied, h)
                for k in range(QB):
                    if k == 2:
                        pe.wait_ge(cks_copied, h + 1 + next_scaled)
                        pe.wait_ge(krs_copied, h + 1 + next_scaled)
                    for q in range(k, QB):
                        t = nc.tensor.transpose(side[:, (2, 3, 0, 1)[k], (q - k) * P:(q - k + 1) * P],
                                                prob[:, h % 2, (P_AT[q] + k) * P:(P_AT[q] + k + 1) * P], ident)
                    t.then_inc(prob_turned, 1)
                for k in range(QB):
                    if k % 2 == 0:
                        pe.wait_ge(prob_t_act, 2 * h + k // 2 + 1)
                    else:
                        pe.wait_ge(prob_t_dve, 2 * h + k // 2 + 1)
                    mm = nc.tensor.matmul(side[:, 2, k * P:SEQ], rows[:, k, 0:KL],
                                          prob_t[:, PT_AT[k] * P:(PT_AT[k] + QB - k) * P], start=(k == 0), stop=(k == QB - 1))
                mm.then_inc(pv_done, 1)
                pe.wait_ge(o_copied, h + 1)
                pe.wait_ge(o_samples, h + 1)
                nc.tensor.matmul(side[:, 3, 0:SEQ], wkv[:, h, :], o_t[:, 0:SEQ], start=True, stop=True)
                nc.tensor.matmul(side[:, 0, 0:NS], wkv[:, h, :], o_t[:, SEQ:TOK], start=True, stop=True).then_inc(uv_done, 1)

            n, e = at_wo.chunk, at_wo.evac
            for half in range(2):
                h0 = half * KC
                if half:
                    pe.wait_ge(evac_done, at_wo.evac + 8)
                scale_keys(h0)
                for h in range(h0, h0 + KC + 1):
                    if h < h0 + KC:
                        scores(h)
                    more = h + 1 < h0 + KC
                    if more:
                        scale_keys(h + 1)
                    if h > h0:
                        values(h - 1, 2 if more else (1 if h < h0 + KC else 0))
                for i in range(4):
                    down(n, e, at_wo.h + h0, KC, slot=i % 2)
                    n, e = n + 1, e + 2
            ffn(at_ffn[3], True)
            for k in range(KD):
                pe.wait_ge(evac_done, at_end.evac - KD + k + 1)
                if k >= 2:
                    pe.wait_ge(out_copied, k - 1)
                for q in range(QB):
                    nc.tensor.transpose(side[:, k % 2, q * P:(q + 1) * P], x[:, k, q * P:(q + 1) * P], ident)
                nc.tensor.transpose(side[0:NS, 2 + k % 2, 0:P], x[:, k, SEQ:TOK], ident).then_inc(out_turned, 1)

        @block.scalar
        def _(act):
            act.dma_start(ws_nat, gmlp_w_s[0].rearrange("g i j -> i g j")).then_inc(ws_in, 16)
            act.dma_start(bs_all[:], gmlp_b_s[0].partition_broadcast(P)).then_inc(ws_in, 16)
            with nc.allow_non_contiguous_dma("a few hundred words"):
                act.dma_start(bs_first[:], gmlp_b_s[0][:, 0].partition_broadcast(P)).then_inc(ws_in, 16)
                act.dma_start(ws_first[:], gmlp_w_s[0][:, 0, 0].partition_broadcast(P)).then_inc(ws_in, 16)

            def split_ahead(n0, i, s, t):
                act.wait_ge(raw_in[1 - s], 16 * (i + n0 // 2 + 1 + s))
                act.wait_ge(tile_done, t + 4 * i + 2 * s)
                nc.scalar.activation(w_hi[:, 1 - s, :], raw[:, 1 - s, :], ACT.Copy).then_inc(hi_done, 1)

            def squares(src, m, before):
                if before >= 2:
                    act.wait_ge(sum_done, before - 1)
                nc.scalar.activation(square[:, m:m + 1, :], src, ACT.Square).then_inc(square_done, 1)

            def norm_tile(norm, k, e, sums):
                act.wait_ge(evac_done, e)
                nc.scalar.activation(xg_hi[:, k, :], x[:, k, :], ACT.Copy,
                                     scale=gain[:, norm, k:k + 1]).then_inc(xg_hi_done, 1)
                squares(x[:, k:k + 1, :], k % 2, sums + k)

            def rms_root(at):
                act.wait_ge(rms_mm, at.rms + 1)
                nc.scalar.activation(halves(root[:, :]), side[:, 0:2, 0:HALF], ACT.Sqrt, scale=1.0 / D,
                                     bias=eps[:, 0:1]).then_inc(root_done, 1)

            def down(at, n, t, e, final):
                for i in range(4):
                    if n + i < last_chunk:
                        split_ahead(n, i // 2, i % 2, t)
                    for m in range(2):
                        if not final:
                            norm_tile(at.norm, 2 * i + m, e + 2 * i + m + 1, at.sums - KD)

            def ffn(at, after, final=False):
                n, t, e, h, a = at.chunk, at.tile, at.evac, at.h, at.act
                for g, pairs in enumerate(FF_GROUPS):
                    def gate_up(i, first=False, n=n, t=t, e=e, h=h):
                        split_ahead(n, i, 0, t)
                        if first:
                            rms_root(at)
                        for m in range(2):
                            act.wait_ge(evac_done, e + 4 * i + m + 1)
                            nc.scalar.activation(tmp_act[:, m, :], tmp_in[:, m, :], ACT.Silu).then_inc(act_done, 1)
                        split_ahead(n, i, 1, t)
                        for m in range(2):
                            act.wait_ge(evac_done, e + 4 * i + m + 3)
                            act.wait_ge(eps_set, 1)
                            nc.scalar.activation(h_hi[:, bass.ds(2 * i + m, 1), :], tmp_h[:, m:m + 1, :],
                                                 ACT.Copy).then_inc(h_hi_done, 1)
                    start = 1 if g == 0 else 0
                    if start:
                        gate_up(0, True)
                    with act.Fori(0, pairs - start) as i:
                        gate_up(i + start)
                    n, t, e = n + 2 * pairs, t + 4 * pairs, e + 4 * pairs
                    if g + 1 < len(FF_GROUPS):
                        with act.Fori(0, 2) as i:
                            for s in range(2):
                                split_ahead(n, i, s, t)
                    else:
                        down(after, n, t, e, final)
                    n, t, e = n + 4, t + 8, e + 8

            act.wait_ge(eps_set, 1)
            act.wait_ge(raw_in[0], 16)
            nc.scalar.activation(w_hi[:, 0, :], raw[:, 0, :], ACT.Copy).then_inc(hi_done, 1)
            for k in range(KD):
                norm_tile(0, k, k + 1, 0)
            for g in range(NG):
                act.wait_ge(ws_turned, g + 1)
                nc.scalar.activation(ws_t[:, g, :], side[:, 2 + g % 2, 0:P], ACT.Copy).then_inc(ws_copied, 1)
            ffn(at_ffn[0], at_gmlp)

            n, t, e, a, sums = at_gmlp.chunk, at_gmlp.tile, at_gmlp.evac, at_gmlp.act, at_gmlp.sums

            def v_chunk(i, s, first=False):
                split_ahead(n, i, s, t)
                if first:
                    rms_root(at_gmlp)
                for m in range(2):
                    j = 4 * i + 2 * s + m
                    act.wait_ge(evac_done, e + j + 1)
                    nc.scalar.activation(v[:, bass.ds(j, 1), :], tmp_in[:, m:m + 1, :], ACT.Gelu_apprx_tanh,
                                         bias=b_in[:, bass.ds(j + GT, 1)]).then_inc(act_done, 1)
                    act.wait_ge(act_done, a + j + 1)
                    squares(v[:, bass.ds(j, 1), :], m, sums + j)
            for c in range(n_v):
                v_chunk(c // 2, c % 2, c == 0)
            n, t, e, a = n + n_v, t + 2 * n_v, e + 2 * n_v, a + GT
            for g in range(NG):
                if g == NG // 2:
                    for i in range(4):
                        split_ahead(n, i // 2, i % 2, t)
                    n, t, e = n + 4, t + 8, e + 8
                split_ahead(n - g % 2, 0, g % 2, t - 2 * (g % 2))
                if g == 0:
                    act.wait_ge(rms_mm, at_gmlp.rms + 2)
                    nc.scalar.activation(rv_root[:, 0:QB + NS], side[:, 2, 0:QB + NS], ACT.Sqrt, scale=1.0 / GM,
                                         bias=eps[:, 0:1])
                    nc.scalar.activation(rv_root[0:NS, QB + NS:QB + NS + 1], side[0:NS, 2, QB + NS:QB + NS + 1],
                                         ACT.Sqrt, scale=1.0 / GM, bias=eps[0:NS, 0:1]).then_inc(root_done, 1)
                for m in range(2):
                    j = 2 * g + m
                    act.wait_ge(evac_done, e + m + 1)
                    if g > 0:
                        act.wait_ge(mul_done, at_gmlp.h + j - 1)
                    nc.scalar.activation(tmp_act[:, m, :], tmp_in[:, m, :], ACT.Gelu_apprx_tanh,
                                         bias=b_in[:, j:j + 1]).then_inc(act_done, 1)
                for m in range(2):
                    j = 2 * g + m
                    act.wait_ge(mul_done, at_gmlp.h + j + 1)
                    nc.scalar.activation(h_hi[:, j % KC, :], tmp_h[:, m, :], ACT.Copy).then_inc(h_hi_done, 1)
                n, t, e = n + 1, t + 2, e + 2
            down(at_ffn[1], n, t, e, False)
            ffn(at_ffn[1], at_ffn[2])
            ffn(at_ffn[2], at_mla)

            def split_next(n, tiles):
                if at_uq.chunk <= n < at_wo.chunk:
                    act.wait_ge(uq_rope_in[n % 2], 48 * ((n - at_uq.chunk) // 2 + 1))
                act.wait_ge(raw_in[n % 2], 16 * (n // 2 + 1))
                act.wait_ge(tile_done, tiles)
                nc.scalar.activation(w_hi[:, n % 2, :], raw[:, n % 2, :], ACT.Copy).then_inc(hi_done, 1)

            n, t, e = at_mla.chunk, at_mla.tile, at_mla.evac
            act.wait_ge(dkv_rope_in, 16)
            split_next(n + 1, t)
            rms_root(at_mla)
            for m in range(2):
                act.wait_ge(evac_done, e + m + 1)
                nc.scalar.activation(square[:, m, :], cq[:, m, :], ACT.Square).then_inc(cq_squared, 1)
            split_next(n + 2, t + 2)
            act.wait_ge(rms_mm, at_mla.rms + 2)
            nc.scalar.activation(halves(root[:, :]), side[:, 0:2, 0:HALF], ACT.Sqrt, scale=1.0 / QL,
                                 bias=eps[:, 0:1]).then_inc(root_done, 1)
            act.wait_ge(evac_done, e + 3)
            nc.scalar.activation(tq[:, 0, :], c_t[:], ACT.Square).then_inc(c_squared, 1)
            for m in range(2):
                act.wait_ge(cqn_set, m + 1)
                nc.scalar.activation(h_hi[:, m, :], cq[:, m, :], ACT.Copy).then_inc(h_hi_done, 1)
            act.wait_ge(rms_mm, at_mla.rms + 3)
            act.wait_ge(rstd_done, at_mla.rms + 2)
            nc.scalar.activation(halves(root[:, :]), side[:, 2:4, 0:HALF], ACT.Sqrt, scale=1.0 / KL,
                                 bias=eps[:, 0:1]).then_inc(root_done, 1)

            n, t, e = at_uq.chunk, at_uq.tile, at_uq.evac
            act.wait_ge(gg_set, 1)
            for u in range(24):
                c, part = u // 6, u % 6
                if part == 0 and c < 3:
                    split_next(n + c + 1, t + 6 * c)
                if u >= 2:
                    act.wait_ge(q_ssq, u - 1)
                act.wait_ge(evac_done, e + u + 1)
                nc.scalar.activation(sq_h[:, u % 2, :], tq[:, u % 2, :], ACT.Square).then_inc(tq_squared, 1)
                if part % 3 != 2:
                    nc.scalar.activation(qn[:, 4 * c + 2 * (part // 3) + part % 3, :], tq[:, u % 2, :], ACT.Copy,
                                         scale=gg[:, 0:1]).then_inc(tq_read, 1)
                else:
                    nc.scalar.activation(few[0:1, 0:1], eps[0:1, 0:1], ACT.Copy).then_inc(tq_read, 1)
            act.wait_ge(q_ssq, 24)
            act.wait_ge(kr_set, 1)
            nc.scalar.activation(sq_h[:, 0, :], kr_t[:], ACT.Square).then_inc(kr_squared, 1)
            for h in range(H):
                act.wait_ge(wuk_turned, h + 1)
                if h >= 2:
                    act.wait_ge(lat_done, h - 1)
                nc.scalar.activation(wuk_t[:, h % 2, :], side[:, h % 2, 0:P], ACT.Copy).then_inc(wuk_copied, 1)
                act.wait_ge(kn_done, h + 1)
                if h >= 2:
                    act.wait_ge(k_ssq, h - 1)
                nc.scalar.activation(halves(sq_h[:, h % 2, :]), main[:, 0, :, 0:HALF], ACT.Square).then_inc(kn_squared, 1)
            for i in range(2):
                act.wait_ge(ssq_set, i + 1)
                if i:
                    act.wait_ge(scale_set, 1)
                nc.scalar.activation(root[:, 0:QB * H], ssq[:, 0:QB * H], ACT.Sqrt, scale=1.0 / QK, bias=eps[:, 0:1])
                nc.scalar.activation(root[0:NS, QB * H:5 * H], ssq[0:NS, QB * H:5 * H], ACT.Sqrt, scale=1.0 / QK,
                                     bias=eps[0:NS, 0:1]).then_inc(ssq_root, 1)
            for k in range(2 * NS):
                act.wait_ge(nat_turned, 2 * k + 2)
                if k >= 2:
                    act.wait_ge(nat_used, k - 1)
                nc.scalar.activation(kt[:, k % 2, 1, :], side[:, 2 * (k % 2) + 1, :], ACT.Copy).then_inc(kt_r_copied, 1)
            act.wait_ge(ks_turned, 1)
            nc.scalar.activation(ks_all[:, :, :].rearrange("p (a b) c -> p a (b c)", a=2), main[:, 1, :, :],
                                 ACT.Copy).then_inc(ks_copied, 1)
            act.wait_ge(sd_max, 2)
            nc.scalar.activation(sd, sd, ACT.Exp, bias=few[:, 1:2], scale=few[:, 10:11],
                                 accum_out=few[:, 2:3]).then_inc(sd_exp, 1)
            act.wait_ge(sd_turned, 1)
            nc.scalar.activation(ks_all[:, :, :].rearrange("p (a b) c -> p a (b c)", a=2), main[:, 1, :, :],
                                 ACT.Copy).then_inc(sd_t_copied, 1)

            n = at_wo.chunk
            split_next(n, at_uq.tile + 18)

            def krs_copy(h):
                act.wait_ge(k_scaled, 2 * h + 2)
                if h >= 2:
                    act.wait_ge(scored, h - 1)
                nc.scalar.activation(krs[:, h % 2, :], side[:, 1, :], ACT.Copy).then_inc(krs_copied, 1)

            for half in range(2):
                h0 = half * KC
                krs_copy(h0)
                for h in range(h0, h0 + KC + 1):
                    if h + 1 < h0 + KC:
                        krs_copy(h + 1)
                    if h < h0 + KC:
                        act.wait_ge(max_done, h + 1)
                        if h >= 2:
                            act.wait_ge(prob_turned, 4 * (h - 1))
                        if h >= 1:
                            act.wait_ge(inv_done, h)
                        for q in range(QB):
                            a = nc.scalar.activation(prob[:, h % 2, P_AT[q] * P:(P_AT[q] + q + 1) * P],
                                                     main[:, q // 2, q % 2, 0:(q + 1) * P], ACT.Exp,
                                                     bias=few[:, 4 + q:5 + q], scale=rq[:, q * H + h:q * H + h + 1],
                                                     accum_out=few[:, 12 + q:13 + q])
                        a.then_inc(exp_done, 1)
                    if h > h0:
                        g = h - 1
                        for k in (0, 2):
                            act.wait_ge(prob_turned, 4 * g + k + 1)
                            nc.scalar.activation(prob_t[:, PT_AT[k] * P:(PT_AT[k] + QB - k) * P],
                                                 side[:, (2, 0)[k // 2], 0:(QB - k) * P], ACT.Copy).then_inc(prob_t_act, 1)
                        act.wait_ge(pv_done, g + 1)
                        nc.scalar.activation(o_t[:, 0:SEQ], side[:, 2, :], ACT.Copy).then_inc(o_copied, 1)
                        act.wait_ge(uv_copied, g + 1)
                        nc.scalar.activation(h_hi[:, g % KC, :], square[:, g % 2, :], ACT.Copy).then_inc(h_hi_done, 1)
                t = at_wo.tile + 8 * half
                if half == 0:
                    for i in range(4):
                        split_next(n + i + 1, t + 2 * i)
                    n += 4
            down(at_ffn[3], n, at_wo.tile + 8, at_wo.evac + 8, False)
            ffn(at_ffn[3], at_end, True)
            for k in range(KD):
                act.wait_ge(out_turned, k + 1)
                nc.scalar.activation(x_tok[:, :, k * P:(k + 1) * P], side[:, k % 2, :].rearrange("p (q c) -> p q c", q=QB),
                                     ACT.Copy)
                nc.scalar.activation(xs_tok[:, k * P:(k + 1) * P], side[0:NS, 2 + k % 2, 0:P],
                                     ACT.Copy).then_inc(out_copied, 1)

        @block.vector
        def _(dve):
            def split_ahead(n0, i, s):
                dve.wait_ge(hi_done, n0 + 2 * i + s + 2)
                nc.vector.tensor_tensor(w_lo[:, 1 - s, :], raw[:, 1 - s, :], w_hi[:, 1 - s, :].bitcast(F32),
                                        ALU.subtract).then_inc(lo_done, 1)

            def rstd(at):
                dve.wait_ge(root_done, at.rms + 1)
                nc.vector.reciprocal(rstd_all[:], root[:]).then_inc(rstd_done, 1)
                dve.wait_ge(rstd_done, at.rms + 1)

            def norm_tile(norm, k):
                dve.wait_ge(xg_hi_done, KD * norm + k + 1)
                nc.vector.scalar_tensor_tensor(xg_lo[:, k, :], x[:, k, :], gain[:, norm, k:k + 1],
                                               xg_hi[:, k, :].bitcast(F32), ALU.mult, ALU.subtract).then_inc(xg_lo_done, 1)

            def scaled(m, t, norm_tmp=None):
                dve.wait_ge(tile_done, t)
                nc.vector.tensor_tensor(halves(tmp_in[:, m, :]), main[:, m, :, 0:HALF], halves(rstd_all[:, :]),
                                        ALU.mult).then_inc(evac_done, 1)

            def add_to_x(k, m, t, scale):
                dve.wait_ge(tile_done, t)
                xk = x[:, bass.ds(k, 1), :].rearrange("p a (h n) -> p (a h) n", h=2)
                nc.vector.scalar_tensor_tensor(xk, main[:, m, :, 0:HALF], scale, xk, ALU.mult, ALU.add).then_inc(evac_done, 1)

            def down(at, n, t, scale, final):
                for i in range(4):
                    if n + i < last_chunk:
                        split_ahead(n, i // 2, i % 2)
                    for m in range(2):
                        add_to_x(2 * i + m, m, t + 2 * i + m + 1, scale)
                        if not final:
                            norm_tile(at.norm, 2 * i + m)

            def down_loop(n, t, scale):
                with dve.Fori(0, 2) as i:
                    for s in range(2):
                        split_ahead(n, i, s)
                        for m in range(2):
                            add_to_x(4 * i + 2 * s + m, m, t + 4 * i + 2 * s + m + 1, scale)

            def ffn(at, after, final=False):
                n, t, h = at.chunk, at.tile, at.mul
                for g, pairs in enumerate(FF_GROUPS):
                    def gate_up(i, first=False, n=n, t=t, h=h):
                        split_ahead(n, i, 0)
                        if first:
                            rstd(at)
                        for m in range(2):
                            scaled(m, t + 4 * i + m + 1)
                        split_ahead(n, i, 1)
                        for m in range(2):
                            dve.wait_ge(tile_done, t + 4 * i + m + 3)
                            dve.wait_ge(mul_done, h + 2 * i + m + 1)
                            nc.vector.tensor_tensor(halves(tmp_h[:, m, :]), main[:, m, :, 0:HALF],
                                                    halves(tmp_mul[:, m, :]), ALU.mult).then_inc(evac_done, 1)
                    start = 1 if g == 0 else 0
                    if start:
                        gate_up(0, True)
                    with dve.Fori(0, pairs - start) as i:
                        gate_up(i + start)
                    n, t, h = n + 2 * pairs, t + 4 * pairs, h + 2 * pairs
                    if g + 1 < len(FF_GROUPS):
                        down_loop(n, t, 0.5)
                    else:
                        down(after, n, t, 0.5, final)
                    n, t = n + 4, t + 8

            nc.vector.memset(eps[:], EPS).then_inc(eps_set, 1)
            dve.wait_ge(vectors_turned, 1)
            nc.vector.tensor_copy(vectors[:, 0:n_vec], side[:, 0, 0:n_vec]).then_inc(vectors_set, 1)
            dve.wait_ge(vectors_set, 1)
            for k in range(KD):
                dve.wait_ge(tile_done, k + 1)
                nc.vector.tensor_copy(x[:, k, 0:SEQ], main[:, k % 2, 0, :])
                nc.vector.tensor_copy(x[:, k, SEQ:TOK], main[:, k % 2, 1, 0:NS]).then_inc(evac_done, 1)
                norm_tile(0, k)
            dve.wait_ge(hi_done, 1)
            nc.vector.tensor_tensor(w_lo[:, 0, :], raw[:, 0, :], w_hi[:, 0, :].bitcast(F32),
                                    ALU.subtract).then_inc(lo_done, 1)
            ffn(at_ffn[0], at_gmlp)

            n, t, a = at_gmlp.chunk, at_gmlp.tile, at_gmlp.act

            def v_chunk(i, s, first=False):
                split_ahead(n, i, s)
                if first:
                    rstd(at_gmlp)
                for m in range(2):
                    j = 4 * i + 2 * s + m
                    if not isinstance(j, int) or j >= 2:
                        dve.wait_ge(act_done, a + j - 1)
                    scaled(m, t + j + 1)
            v_chunk(0, 0, True)
            v_chunk(0, 1)
            with dve.Fori(0, n_v // 2 - 1) as i:
                v_chunk(i + 1, 0)
                v_chunk(i + 1, 1)
            n, t, a = n + n_v, t + 2 * n_v, a + GT

            def v_times_gain(g):
                vg = v[:, 2 * g:2 * g + 2, :]
                nc.vector.tensor_tensor(vg, vg, bc(v_gain[:, 2 * g:2 * g + 2], TOK), ALU.mult).then_inc(vg_done, 2)

            dve.wait_ge(square_done, at_gmlp.sums + GT)
            v_times_gain(0)
            for g in range(NG):
                if g == NG // 2:
                    down_loop(n, t, 1.0)
                    n, t = n + 4, t + 8
                split_ahead(n - g % 2, 0, g % 2)
                if g == 0:
                    dve.wait_ge(root_done, at_gmlp.rms + 2)
                    nc.vector.reciprocal(rv[:, 0:QB + NS], rv_root[:, 0:QB + NS])
                    nc.vector.reciprocal(rv[0:NS, QB + NS:QB + NS + 1],
                                         rv_root[0:NS, QB + NS:QB + NS + 1]).then_inc(rstd_done, 1)
                    dve.wait_ge(rstd_done, at_gmlp.rms + 2)
                dve.wait_ge(v_turned, g + 1)
                for m in range(2):
                    nc.vector.tensor_tensor(v_tok[:, m, :, :], side[:, m, :].rearrange("p (q c) -> p q c", q=QB),
                                            bc(rv[:, 0:QB], P), ALU.mult).then_inc(v_copied, 1)
                if g >= 2:
                    dve.wait_ge(vs_out[g % 2], 16 * (g // 2))
                nc.vector.tensor_scalar(vs_tok[:, g % 2, :, :], side[0:NS, 2, 0:2 * P].rearrange("p (m c) -> p m c", m=2),
                                        rv[0:NS, QB + NS:QB + NS + 1], None, ALU.mult).then_inc(v_seen, 1)
                dve.wait_ge(vg_done, 2 * g + 2)
                if g > 0:
                    dve.wait_ge(mul_done, at_gmlp.h + 2 * g)
                sm = tmp_mul[:, :, SEQ:TOK]
                nc.vector.scalar_tensor_tensor(sm, v[:, 2 * g:2 * g + 2, SEQ:TOK], ws_first[:, g:g + 1],
                                               rv[:, QB:QB + NS].unsqueeze(1).to_broadcast([P, 2, NS]),
                                               ALU.mult, ALU.mult).then_inc(sample_mix, 1)
                dve.wait_ge(sample_mix, g + 1)
                nc.vector.tensor_scalar(sm, sm, bs_first[:, g:g + 1], None, ALU.add)
                if g + 1 < NG:
                    v_times_gain(g + 1)
                for m in range(2):
                    dve.wait_ge(act_done, a + 2 * g + m - 1)
                    scaled(m, t + m + 1)
                for m in range(2):
                    dve.wait_ge(mix_done, 2 * g + m + 1)
                    bank = (3, 0)[m]
                    nc.vector.tensor_tensor(tmp_mul[:, m, 0:SEQ].rearrange("p (q c) -> p q c", q=QB),
                                            side[:, bank, :].rearrange("p (q c) -> p q c", q=QB),
                                            bs_all[:, g:g + 1, :].to_broadcast([P, QB, P]), ALU.add).then_inc(mixed, 1)
                n, t = n + 1, t + 2
            down(at_ffn[1], n, t, 1.0, False)
            ffn(at_ffn[1], at_ffn[2])
            ffn(at_ffn[2], at_mla)

            def split_next(n):
                dve.wait_ge(hi_done, n + 1)
                nc.vector.tensor_tensor(w_lo[:, n % 2, :], raw[:, n % 2, :], w_hi[:, n % 2, :].bitcast(F32),
                                        ALU.subtract).then_inc(lo_done, 1)

            def scaled_to(dst, m, t):
                dve.wait_ge(tile_done, t)
                nc.vector.tensor_tensor(halves(dst), main[:, m, :, 0:HALF], halves(rstd_all[:, :]),
                                        ALU.mult).then_inc(evac_done, 1)

            n, t = at_mla.chunk, at_mla.tile
            split_next(n + 1)
            rstd(at_mla)
            nc.vector.tensor_tensor(gg[:, 0:1], nope_gains[:, 0:1], nope_gains[:, 1:2], ALU.mult)
            nc.vector.tensor_tensor(gg[:, 1:2], rope_gains[:, 0:1], rope_gains[:, 1:2], ALU.mult).then_inc(gg_set, 1)
            scaled_to(cq[:, 0, :], 0, t + 1)
            scaled_to(cq[:, 1, :], 1, t + 2)
            split_next(n + 2)
            scaled_to(c_t[:, :], 0, t + 3)
            inv = square_sum
            dve.wait_ge(root_done, at_mla.rms + 2)
            nc.vector.reciprocal(inv[:], root[:]).then_inc(rstd_done, 1)
            dve.wait_ge(rstd_done, at_mla.rms + 2)
            for m in range(2):
                nc.vector.scalar_tensor_tensor(cq[:, m, :], cq[:, m, :], q_gain[:, m:m + 1], inv[:], ALU.mult,
                                               ALU.mult).then_inc(cqn_set, 1)
            scaled_to(kr_raw, 1, t + 4)
            dve.wait_ge(kv_in, 32)
            dve.wait_ge(gg_set, 1)
            nc.vector.tensor_scalar(trig_g[:], trig[:], gg[:, 1:2], None, ALU.mult).then_inc(trig_set, 1)
            dve.wait_ge(root_done, at_mla.rms + 3)
            dve.wait_ge(cqn_set, 2)
            nc.vector.reciprocal(inv[:], root[:]).then_inc(rstd_done, 1)
            dve.wait_ge(rstd_done, at_mla.rms + 3)
            nc.vector.scalar_tensor_tensor(c_t[:], c_t[:], kv_gain, inv[:], ALU.mult, ALU.mult).then_inc(c_set, 1)
            dve.wait_ge(kr_swapped, 1)
            nc.vector.tensor_tensor(halves(rope_b[:, :]), side[:, 0:2, 0:HALF], halves(trig[:, 1, :]),
                                    ALU.mult).then_inc(rope_b_set, 1)
            nc.vector.tensor_tensor(kr_t[:], kr_raw, trig[:, 0, :], ALU.mult).then_inc(kr_part, 1)
            dve.wait_ge(rope_b_set, 1)
            dve.wait_ge(kr_part, 1)
            nc.vector.tensor_tensor(kr_t[:], kr_t[:], rope_b[:], ALU.add).then_inc(kr_set, 1)

            n, t = at_uq.chunk, at_uq.tile
            for u in range(24):
                c, part = u // 6, u % 6
                if part == 0 and c < 3:
                    split_next(n + c + 1)
                if u >= 2:
                    dve.wait_ge(tq_read, u - 1)
                    if (u - 2) % 3 == 2:
                        dve.wait_ge(rope_a_set, (u - 2) // 3 + 1)
                dve.wait_ge(tile_done, t + u + 1)
                nc.vector.tensor_copy(halves(tq[:, u % 2, :]), main[:, u % 2, :, 0:HALF]).then_inc(evac_done, 1)
                if part % 3 == 2:
                    r_ = 2 * c + part // 3
                    dve.wait_ge(swapped, r_ + 1)
                    if r_ >= 1:
                        dve.wait_ge(qr_set, r_)
                    else:
                        dve.wait_ge(kr_set, 1)
                        dve.wait_ge(trig_set, 1)
                    nc.vector.tensor_tensor(halves(rope_b[:, :]), side[:, 0:2, 0:HALF], halves(trig_g[:, 1, :]),
                                            ALU.mult).then_inc(rope_b_set, 1)
            for b in range(QB + 1):
                w = P if b < QB else NS
                dve.wait_ge(row_turned, b + 1)
                dst = rows[:, b, :] if b < QB else rows_s[:, :]
                nc.vector.tensor_copy(dst[:, 0:KL + ROPE], side[0:w, b % 2, 0:KL + ROPE])
                if b < QB:
                    nc.vector.tensor_copy(kr_tok[:, b, :], side[:, b % 2, P:2 * P]).then_inc(row_copied, 1)
                else:
                    nc.vector.tensor_copy(few[0:NS, 22:23], side[0:NS, b % 2, 0:1]).then_inc(row_copied, 1)

            def scales(i, bank, extra):
                if i:
                    dve.wait_ge(ssq_root, 1)
                for r0, r1, a, b in ((0, P, 0, QB * H), (0, NS, QB * H, 5 * H)):
                    nc.vector.tensor_copy(extra(r0, r1, a, b)[0], extra(r0, r1, a, b)[1]).then_inc(rope_part, 1)
                dve.wait_ge(rope_part, 4 * i + 2)
                for r0, r1, a, b in ((0, P, 0, QB * H), (0, NS, QB * H, 5 * H)):
                    nb = (b - a) // H
                    other = ssq[r0:r1, a:b].rearrange("p (b h) -> p b h", h=H) if i == 0 else bc(krq[r0:r1, a // H:b // H], H)
                    nc.vector.tensor_tensor(ssq[r0:r1, a:b].rearrange("p (b h) -> p b h", h=H),
                                            side[r0:r1, bank, a:b].rearrange("p (b h) -> p b h", h=H), other,
                                            ALU.add).then_inc(rope_part, 1)

            def scales_end(i, dst):
                dve.wait_ge(ssq_root, i + 1)
                nc.vector.reciprocal(dst[:, 0:QB * H], root[:, 0:QB * H])
                nc.vector.reciprocal(dst[0:NS, QB * H:5 * H], root[0:NS, QB * H:5 * H]).then_inc(scale_set, 1)
                dve.wait_ge(scale_set, i + 1)

            dve.wait_ge(q_ssq, 24)
            scales(0, 2, lambda r0, r1, a, b: (ssq[r0:r1, a:b], side[r0:r1, 2, 5 * H + a:5 * H + b]))
            dve.wait_ge(rope_part, 4)
            nc.vector.tensor_copy(few[:, 23:24], eps[:]).then_inc(ssq_set, 1)
            for h in range(H):
                dve.wait_ge(lat_done, h + 1)
                nc.vector.tensor_copy(halves(qn[:, h, :]), main[:, 1, :, 0:HALF]).then_inc(lat_copied, 1)
            scales_end(0, rq)
            nc.vector.tensor_scalar(rq[:, 0:QB * H], rq[:, 0:QB * H], QK ** -0.5, None, ALU.mult)
            nc.vector.tensor_scalar(rq[0:NS, QB * H:5 * H], rq[0:NS, QB * H:5 * H], QK ** -0.5, None,
                                    ALU.mult).then_inc(q_ssq_read, 1)
            dve.wait_ge(k_ssq, H)
            scales(1, 3, lambda r0, r1, a, b: (krq[r0:r1, a // H:b // H], side[r0:r1, 3, 5 * H + a // H:5 * H + b // H]))
            dve.wait_ge(rope_part, 8)
            nc.vector.tensor_copy(few[:, 23:24], eps[:]).then_inc(ssq_set, 1)
            scales_end(1, ks)
            nc.vector.tensor_copy(rows[:, :, KL + ROPE:CD], ks[:, 0:QB * H].rearrange("p (b h) -> p b h", h=H))
            nc.vector.tensor_copy(rows_s[:, KL + ROPE:CD], ks[0:NS, QB * H:5 * H]).then_inc(rows_done, 1)
            dve.wait_ge(qpad_zero, 1)
            dve.wait_ge(lat_copied, H)
            nc.vector.tensor_copy(q_all[:, 0, :].rearrange("p (b h) -> p b h", h=H),
                                  qn[:, :, SEQ:TOK].rearrange("p h b -> p b h"))
            for odd in range(2):
                lo = ROPE * odd
                nc.vector.tensor_copy(
                    q_all[lo:lo + ROPE, 1, :].rearrange("p (b g t) -> p b g t", g=H // 2, t=2)[:, :, :, odd],
                    qr[lo:lo + ROPE, :, SEQ:TOK].rearrange("p g b -> p b g")).then_inc(q_all_set, 1)
            dve.wait_ge(q_all_set, 2)
            for b in range(NS):
                a = nc.vector.tensor_copy(q_pad[:, :, b, b * H:(b + 1) * H], q_all[:, :, b * H:(b + 1) * H])
            a.then_inc(q_pad_set, 1)
            dve.wait_ge(q_ssq_read, 1)
            nc.vector.tensor_copy(ks_new[:, 0, :].rearrange("p (b h) -> p b h", h=H),
                                  ks[0:NS, QB * H:5 * H].unsqueeze(1).to_broadcast([NS, NS, H])).then_inc(ks_new_set, 1)
            nc.vector.tensor_tensor(ks_new[:, 1, :].rearrange("p (b h) -> p b h", h=H),
                                    own_rows.rearrange("p (b h) -> p b h", h=H),
                                    rq[0:NS, QB * H:5 * H].unsqueeze(1).to_broadcast([NS, NS, H]),
                                    ALU.mult).then_inc(ks_new_set, 1)
            for k in range(2 * NS):
                dve.wait_ge(nat_turned, 2 * k + 1)
                if k >= 2:
                    dve.wait_ge(nat_used, k - 1)
                nc.vector.tensor_copy(kt[:, k % 2, 0, :], side[:, 2 * (k % 2), :]).then_inc(kt_c_copied, 1)
            dve.wait_ge(nat_used, 2 * NS)
            dve.wait_ge(ks_copied, 1)
            nc.vector.tensor_tensor(sd[:, 0:PAST].rearrange("p (a c) -> p a c", a=2), main[:, 0, :, :],
                                    ks_all[:, :, :].rearrange("p (a b) c -> p a (b c)", a=2), ALU.mult)
            dve.wait_ge(new_scored, 1)
            nc.vector.tensor_copy(few[:, 10:11], side[:, 2, 0:1])
            nc.vector.tensor_copy(krq_s, side[:, 1, 0:NS]).then_inc(new_ready, 1)
            dve.wait_ge(new_ready, 1)
            nc.vector.tensor_tensor(sd[:, PAST:PAST + NS], side[:, 0, 0:NS], krq_s, ALU.mult).then_inc(new_ready, 1)
            dve.wait_ge(new_ready, 2)
            nc.vector.tensor_tensor(sd[:, PAST:PAST + NS], sd[:, PAST:PAST + NS], own, ALU.add).then_inc(sd_set, 1)
            dve.wait_ge(sd_set, 1)
            nc.vector.tensor_reduce(few[:, 0:1], sd, AX.X, ALU.max).then_inc(sd_max, 1)
            dve.wait_ge(sd_max, 1)
            nc.vector.tensor_scalar(few[:, 1:2], few[:, 0:1], few[:, 10:11], -1.0, ALU.mult, ALU.mult).then_inc(sd_max, 1)
            dve.wait_ge(sd_exp, 1)
            nc.vector.reciprocal(few[:, 3:4], few[:, 2:3]).then_inc(sd_inv, 1)
            dve.wait_ge(sd_inv, 1)
            nc.vector.tensor_scalar(sd, sd, few[:, 3:4], None, ALU.mult).then_inc(sd_prob, 1)
            dve.wait_ge(sd_turned, 1)
            nc.vector.tensor_copy(p_new, side[0:NS, 3, 0:P]).then_inc(sd_t_copied, 1)
            dve.wait_ge(os_done, 1)
            nc.vector.tensor_copy(o_s[:], main[:, 0, 0, 0:P]).then_inc(os_copied, 1)

            split_next(at_wo.chunk)
            n = at_wo.chunk

            def diagonal(h):
                if h >= 1:
                    dve.wait_ge(k_scaled, 2 * h)
                kh = ks[:, 0:QB * H].rearrange("p (b h) -> p b h", h=H)[:, :, h]
                nc.vector.tensor_tensor(diag[:], ident.unsqueeze(1).to_broadcast([P, QB, P]), bc(kh, P),
                                        ALU.mult).then_inc(diag_set, 1)

            def cks_copy(h):
                dve.wait_ge(k_scaled, 2 * h + 1)
                if h >= 2:
                    dve.wait_ge(scored, h - 1)
                nc.vector.tensor_copy(cks[:, h % 2, :], side[:, 0, :]).then_inc(cks_copied, 1)

            for half in range(2):
                h0 = half * KC
                diagonal(h0)
                cks_copy(h0)
                diagonal(h0 + 1)
                for h in range(h0, h0 + KC + 1):
                    if h < h0 + KC:
                        dve.wait_ge(scored, h + 1)
                        for q in range(QB):
                            a = nc.vector.tensor_reduce(few[:, 16 + q:17 + q], main[:, q // 2, q % 2, 0:(q + 1) * P], AX.X,
                                                        ALU.max)
                        a.then_inc(max_set, 1)
                        dve.wait_ge(max_set, h + 1)
                        if h >= 1:
                            dve.wait_ge(exp_done, h)
                        rh = rq[:, 0:QB * H].rearrange("p (b h) -> p b h", h=H)[:, :, h]
                        nc.vector.scalar_tensor_tensor(few[:, 4:4 + QB], few[:, 16:16 + QB], -1.0, rh, ALU.mult,
                                                       ALU.mult).then_inc(max_done, 1)
                    if h + 1 < h0 + KC:
                        cks_copy(h + 1)
                        if h + 2 < h0 + KC:
                            diagonal(h + 2)
                    if h > h0:
                        g = h - 1
                        for k in (1, 3):
                            dve.wait_ge(prob_turned, 4 * g + k + 1)
                            nc.vector.tensor_copy(prob_t[:, PT_AT[k] * P:(PT_AT[k] + QB - k) * P],
                                                  side[:, (3, 1)[k // 2], 0:(QB - k) * P]).then_inc(prob_t_dve, 1)
                        dve.wait_ge(uv_done, g + 1)
                        if g >= 2:
                            dve.wait_ge(h_lo_done, at_wo.h + g - 1)
                        nc.vector.tensor_copy(square[:, g % 2, 0:SEQ], side[:, 3, :])
                        nc.vector.tensor_copy(square[:, g % 2, SEQ:TOK], side[:, 0, 0:NS]).then_inc(uv_copied, 1)
                    if h < h0 + KC:
                        dve.wait_ge(exp_done, h + 1)
                        if h >= 1:
                            dve.wait_ge(prob_done, h)
                        nc.vector.reciprocal(inv_sum, few[:, 12:12 + QB]).then_inc(inv_done, 1)
                t = at_wo.tile + 8 * half
                if half == 0:
                    down_loop(n, t, 1.0)
                    n += 4
            down(at_ffn[3], n, at_wo.tile + 8, 1.0, False)
            ffn(at_ffn[3], at_end, True)

        @block.gpsimd
        def _(pool):
            def add_squares(m, before, first):
                pool.wait_ge(square_done, before + 1)
                if first:
                    nc.gpsimd.tensor_copy(square_sum[:], square[:, m, :]).then_inc(sum_done, 1)
                else:
                    pool.wait_ge(sum_done, before)
                    nc.gpsimd.tensor_tensor(square_sum[:], square_sum[:], square[:, m, :], ALU.add).then_inc(sum_done, 1)

            def h_rest(m, f, h):
                pool.wait_ge(h_hi_done, h)
                if not isinstance(h, int):
                    pool.wait_ge(ws_masked, 1)
                nc.gpsimd.tensor_tensor(h_lo[:, bass.ds(f, 1), :], tmp_h[:, m:m + 1, :],
                                        h_hi[:, bass.ds(f, 1), :].bitcast(F32), ALU.subtract).then_inc(h_lo_done, 1)

            def ffn(at, after, final=False):
                h, a = at.h, at.act
                for g, pairs in enumerate(FF_GROUPS):
                    with pool.Fori(0, pairs) as i:
                        for m in range(2):
                            pool.wait_ge(act_done, a + 2 * i + m + 1)
                            nc.gpsimd.tensor_tensor(tmp_mul[:, m, :], tmp_act[:, m, :], rstd_all[:],
                                                    ALU.mult).then_inc(mul_done, 1)
                        for m in range(2):
                            h_rest(m, 2 * i + m, h + 2 * i + m + 1)
                    h, a = h + 2 * pairs, a + 2 * pairs
                if not final:
                    for k in range(KD):
                        add_squares(k % 2, after.sums - KD + k, k == 0)

            for k in range(KD):
                add_squares(k % 2, k, k == 0)
            pool.wait_ge(ws_in, 16 * 4)
            nc.gpsimd.affine_select(out=ws_nat, in_=ws_nat, compare_op=ALU.is_ge, fill=0.0, base=0,
                                    pattern=[[0, NG], [-1, P]], channel_multiplier=1).then_inc(ws_masked, 1)
            ffn(at_ffn[0], at_gmlp)

            add_squares(0, at_gmlp.sums, True)
            add_squares(1, at_gmlp.sums + 1, False)
            with pool.Fori(0, GT // 2 - 1) as i:
                for m in range(2):
                    add_squares(m, at_gmlp.sums + 2 * i + 2 + m, False)
            for g in range(NG):
                pool.wait_ge(v_seen, g + 1)
                pool.dma_start(new_v[0, :, 0, 2 * g * P:2 * (g + 1) * P], vs_tok[:, g % 2, :, :].rearrange("p m c -> p (m c)"))\
                    .then_inc(vs_out[g % 2], 16)
                for m in range(2):
                    j = 2 * g + m
                    pool.wait_ge(act_done, at_gmlp.act + GT + j + 1)
                    pool.wait_ge(mixed, j + 1)
                    if g > 0:
                        pool.wait_ge(h_lo_done, at_gmlp.h + j - 1)
                    nc.gpsimd.tensor_tensor(tmp_h[:, m, :], tmp_act[:, m, :], tmp_mul[:, m, :],
                                            ALU.mult).then_inc(mul_done, 1)
                for m in range(2):
                    h_rest(m, (2 * g + m) % KC, at_gmlp.h + 2 * g + m + 1)
            for s in range(2):
                pool.wait_ge(vs_out[s], 16 * NG // 2)
            for k in range(KD):
                add_squares(k % 2, at_ffn[1].sums - KD + k, k == 0)
            ffn(at_ffn[1], at_ffn[2])
            ffn(at_ffn[2], at_mla)

            for m in range(2):
                pool.wait_ge(h_hi_done, at_mla.h + m + 1)
                nc.gpsimd.tensor_tensor(h_lo[:, m, :], cq[:, m, :], h_hi[:, m, :].bitcast(F32),
                                        ALU.subtract).then_inc(h_lo_done, 1)
            pool.wait_ge(trig_set, 1)
            pool.wait_ge(kr_set, 1)
            for r_ in range(H // 2):
                u = 3 * r_ + 2
                pool.wait_ge(evac_done, at_uq.evac + u + 1)
                if r_:
                    pool.wait_ge(qr_set, r_)
                nc.gpsimd.tensor_tensor(rope_a[:], tq[:, u % 2, :], trig_g[:, 0, :], ALU.mult).then_inc(rope_a_set, 1)
                pool.wait_ge(rope_b_set, r_ + 2)
                pool.wait_ge(rope_a_set, r_ + 1)
                nc.gpsimd.tensor_tensor(qr[:, r_, :], rope_a[:], rope_b[:], ALU.add).then_inc(qr_set, 1)
            pool.wait_ge(lat_done, H)
            pool.wait_ge(k_ssq, H)
            pool.wait_ge(qr_set, H // 2)
            nc.gpsimd.memset(q_all[:, 1, :], 0.0)
            nc.gpsimd.memset(q_pad[:], 0.0).then_inc(qpad_zero, 1)
            for k in range(2 * NS):
                pool.wait_ge(nat_in[k % 2], 64 * (k // 2 + 1))
                if k >= 2:
                    pool.wait_ge(nat_turned, 2 * (k - 1))
                b, j = k // 2, 4 * (k % 2)
                for a in range(2):
                    nc.gpsimd.tensor_copy(kr_dup[:, k % 2, :, a * ROPE:(a + 1) * ROPE], nat[:, k % 2, :, KL:KL + ROPE])
                nc.gpsimd.tensor_copy(ks_all[:, j:j + 4, b * H:(b + 1) * H], nat[:, k % 2, :, KL + ROPE:CD]).then_inc(nat_dup, 1)
            pool.wait_ge(os_copied, 1)
            for half in range(2):
                h0 = half * KC
                for h in range(h0, h0 + KC + 1):
                    if h > h0:
                        g = h - 1
                        if g >= 1:
                            pool.wait_ge(uv_done, g)
                        nc.gpsimd.tensor_copy(o_t[:, SEQ:TOK], o_s[:, :].rearrange("p (b h) -> p b h", h=H)[:, :, g])\
                            .then_inc(o_samples, 1)
                        pool.wait_ge(h_hi_done, at_wo.h + g + 1)
                        nc.gpsimd.tensor_tensor(h_lo[:, g % KC, :], square[:, g % 2, :], h_hi[:, g % KC, :].bitcast(F32),
                                                ALU.subtract).then_inc(h_lo_done, 1)
                    if h < h0 + KC:
                        pool.wait_ge(inv_done, h + 1)
                        for q in range(QB):
                            pq = prob[:, h % 2, P_AT[q] * P:(P_AT[q] + q + 1) * P]
                            a = nc.gpsimd.tensor_scalar(pq, pq, inv_sum[:, q:q + 1], None, ALU.mult)
                        a.then_inc(prob_done, 1)
            for k in range(KD):
                add_squares(k % 2, at_ffn[3].sums - KD + k, k == 0)
            ffn(at_ffn[3], at_end, True)


INPUTS = ("x_prompt", "x_sample", "cache_mla", "page_table", "norm_g", "ffn_w_gate", "ffn_w_up", "ffn_w_down",
          "gmlp_w_in", "gmlp_b_in", "gmlp_v_norm", "gmlp_w_s", "gmlp_b_s", "gmlp_w_out",
          "mla_w_dq", "mla_q_norm", "mla_w_uq", "mla_w_dkv", "mla_kv_norm", "mla_w_uk", "mla_w_uv",
          "mla_qk_gain_q", "mla_qk_gain_k", "mla_w_o")
OUTPUTS = ((1, SEQ, D), (NS, 1, D), (1, 1, SEQ, CD), (1, NS, 1, CD), (1, NS, 1, GM))


def kernel(**inputs):
    import concourse.bacc as bacc
    from concourse.bass_utils import run_bass_kernel_spmd

    nc = bacc.Bacc("TRN2", target_bir_lowering=False, num_devices=1)
    arrays, args = {}, []
    for name in INPUTS:
        a = np.ascontiguousarray(inputs[name])
        arrays[f"in_{name}"] = a
        args.append(nc.dram_tensor(f"in_{name}", a.shape, mybir.dt.from_np(a.dtype), kind="ExternalInput").ap())
    for i, shape in enumerate(OUTPUTS):
        args.append(nc.dram_tensor(f"out_{i}", shape, F32, kind="ExternalOutput").ap())
    program(nc, *args)
    r = run_bass_kernel_spmd(nc, [arrays], core_ids=[0])
    return tuple(r.results[0][f"out_{i}"] for i in range(len(OUTPUTS)))
```

```python
from contextlib import ExitStack

import numpy as np

import concourse.bass as bass
from concourse import mybir

P = 128
F32, F32R, I32 = mybir.dt.float32, mybir.dt.float32r, mybir.dt.int32
ALU, ACT, AX = mybir.AluOpType, mybir.ActivationFunctionType, mybir.AxisListType

SEQ, NS = 512, 8
TOK = SEQ + NS
HALF = TOK // 2
QB = SEQ // P
D = 1024
KD = D // P
FF = 2816
FF_GROUPS = (4, 4, 3)
GM = 2048
GT = GM // P
NG = 8
H, QL, KL, NOPE, ROPE, VD = 16, 256, 128, 128, 64, 128
QK = NOPE + ROPE
CD = KL + ROPE + H
PAST, PAGE = 1024, 128
NP = PAST // PAGE
POOL = 80
THETA = 10000.0
EPS = 1e-6
NEG = -1e30
KC = 8
WC = 256
SLOT = KC * WC


def constants():
    ident = np.eye(P, dtype=np.float32)
    ones = np.ones((P, P), np.float32)
    r = np.arange(P)
    swap = np.zeros((P, P), np.float32)
    swap[r, r ^ (ROPE // 2)] = 1.0
    causal = np.where(r[None, :] > r[:, None], np.float32(NEG), np.float32(0.0))
    own = np.where(r[:, None] // H == np.arange(NS)[None, :], np.float32(0.0), np.float32(NEG))
    own_rows = np.zeros((P, P), np.float32)
    own_rows[:NS] = (np.arange(NS)[:, None] == r[None, :] // H)
    two = (r[:, None] // ROPE == np.arange(2)[None, :]).astype(np.float32)
    half = ROPE // 2
    inv = np.float32(THETA) ** (-np.arange(half, dtype=np.float32) / np.float32(half))
    pos = np.concatenate([np.arange(SEQ), np.full(NS, PAST)]).astype(np.float32)
    ang = inv[r % half][:, None] * pos[None, :]
    cos = np.cos(ang).astype(np.float32)
    sin = np.sin(ang).astype(np.float32) * np.where(r % ROPE < half, -1.0, 1.0).astype(np.float32)[:, None]
    return np.concatenate([ident, ones, swap, causal, own, own_rows, two, cos, sin], axis=1).astype(np.float32)


N_CONST = 4 * P + NS + P + 2
N_TRIG = 2 * TOK


class At:

    FIELDS = ("chunk", "tile", "evac", "h", "mul", "act", "norm", "rms", "sums")

    def __init__(self, **counts):
        self.chunk, self.tile, self.evac, self.h, self.mul, self.act, self.norm, self.rms, self.sums = (
            counts.get(f, 0) for f in self.FIELDS)

    def past(self, chunk=0, tile=0, evac=0, h=0, mul=0, act=0, norm=0, rms=0, sums=0):
        return At(chunk=self.chunk + chunk, tile=self.tile + tile, evac=self.evac + evac, h=self.h + h,
                  mul=self.mul + mul, act=self.act + act, norm=self.norm + norm, rms=self.rms + rms, sums=self.sums + sums)


def ffn_past(at, last=False):
    pairs = sum(FF_GROUPS)
    chunks = 2 * pairs + 4 * len(FF_GROUPS)
    return at.past(chunks, 2 * chunks, 2 * chunks, 2 * pairs, 2 * pairs, 2 * pairs, 1, 1, 0 if last else KD)


def bc(ap, n):
    return ap.unsqueeze(len(ap.shape)).to_broadcast(list(ap.shape) + [n])


def halves(ap):
    return ap.rearrange("p (h n) -> p h n", h=2)


def program(nc, x_prompt, x_sample, cache_mla, page_table, norm_g, ffn_w_gate, ffn_w_up, ffn_w_down,
            gmlp_w_in, gmlp_b_in, gmlp_v_norm, gmlp_w_s, gmlp_b_s, gmlp_w_out,
            mla_w_dq, mla_q_norm, mla_w_uq, mla_w_dkv, mla_kv_norm, mla_w_uk, mla_w_uv,
            mla_qk_gain_q, mla_qk_gain_k, mla_w_o,
            y_prompt, y_sample, new_prompt, new_sample, new_v):
    table = nc.inline_tensor(constants(), name="shape_constants").ap()

    with ExitStack() as ctx:
        def sb(name, shape, dt=F32, at=ctx):
            return at.enter_context(nc.sbuf_tensor(name, shape, dt))

        def sem(name):
            return ctx.enter_context(nc.semaphore(name))

        x = sb("x", [P, KD, TOK])
        operands = ExitStack()
        raw = sb("raw", [P, 2, SLOT], F32, operands)
        h_hi = sb("h_hi", [P, KC, TOK], F32R, operands)
        h_lo = sb("h_lo", [P, KC, TOK], F32R, operands)
        w_hi = sb("w_hi", [P, 2, SLOT], F32R, operands)
        w_lo = sb("w_lo", [P, 2, SLOT], F32R, operands)
        operands.close()
        over = sb("over", [P, 6 * SLOT + 2 * KC * TOK])
        rstd_all = sb("rstd_all", [P, TOK])
        square = sb("square", [P, 2, TOK])
        square_sum = sb("square_sum", [P, TOK])
        root = sb("root", [P, TOK])
        const = sb("const", [P, N_CONST])
        eps = sb("eps", [P, 1])
        vectors = sb("vectors", [P, P])
        ident, ones, swap, causal = (const[:, i * P:(i + 1) * P] for i in range(4))
        own = const[:, 4 * P:4 * P + NS]
        own_rows = const[0:NS, 4 * P + NS:5 * P + NS]
        two = const[:, 5 * P + NS:5 * P + NS + 2]
        n_gain, n_bias, n_vg = 6 * KD, 2 * GT, GT
        gain = vectors[:, 0:n_gain].rearrange("p (n k) -> p n k", k=KD)
        b_in = vectors[:, n_gain:n_gain + n_bias]
        v_gain = vectors[:, n_gain + n_bias:n_gain + n_bias + n_vg]
        c0 = n_gain + n_bias + n_vg
        q_gain, kv_gain = vectors[:, c0:c0 + 2], vectors[:, c0 + 2:c0 + 3]
        nope_gains, rope_gains = vectors[:, c0 + 3:c0 + 5], vectors[:, c0 + 5:c0 + 7]
        n_vec = c0 + 7

        early = ExitStack()
        xg_hi = sb("xg_hi", [P, KD, TOK], F32R, early)
        xg_lo = sb("xg_lo", [P, KD, TOK], F32R, early)
        wide = ExitStack()
        v = sb("v", [P, GT, TOK], F32, wide)
        tmp_in = sb("tmp_in", [P, 2, TOK], F32, wide)
        tmp_act = sb("tmp_act", [P, 2, TOK], F32, wide)
        tmp_mul = sb("tmp_mul", [P, 2, TOK], F32, wide)
        tmp_h = sb("tmp_h", [P, 2, TOK], F32, wide)
        ws_t = sb("ws_t", [P, NG, P], F32, wide)
        bs_all = sb("bs_all", [P, NG, P], F32, wide)
        v_tok = sb("v_tok", [P, 2, QB, P], F32, wide)
        vs_tok = sb("vs_tok", [NS, 2, 2, P], F32, wide)
        ws_first = sb("ws_first", [P, NG], F32, wide)
        bs_first = sb("bs_first", [P, NG], F32, wide)
        rv_root = sb("rv_root", [P, QB + 1 + NS], F32, wide)
        rv = sb("rv", [P, QB + 1 + NS], F32, wide)
        x_tok = v[:, 0:8, :].rearrange("p a n -> p (a n)")[:, 0:QB * D].rearrange("p (q d) -> p q d", q=QB)
        xs_tok = v[0:NS, 8:10, :].rearrange("p a n -> p (a n)")[:, 0:D]
        vector_rows = v[:, 12, 0:P]
        ws_nat = v_tok[:, :, :, :].rearrange("p a q d -> p (a q) d")
        wide.close()
        early.close()

        late = ExitStack()
        qn = sb("qn", [P, H, TOK], F32, late)
        qr = sb("qr", [P, H // 2, TOK], F32, late)
        wkv = sb("wkv", [P, H, P], F32, late)
        c_t = sb("c_t", [P, TOK], F32, late)
        kr_t = sb("kr_t", [P, TOK], F32, late)
        rows = sb("rows", [P, QB, CD], F32, late)
        rows_s = sb("rows_s", [NS, CD], F32, late)
        ks_hi = sb("ks_hi", [H, SEQ], F32R, late)
        ks_lo = sb("ks_lo", [H, SEQ], F32R, late)
        pick = sb("pick", [H, H], F32R, late)
        mask_ops = sb("mask_ops", [P, 2, P], mybir.dt.bfloat16, late)
        ssq = sb("ssq", [P, 5 * H], F32, late)
        rq = sb("rq", [P, 5 * H], F32, late)
        ks = sb("ks", [P, 5 * H], F32, late)
        krq = sb("krq", [P, 5], F32, late)
        gg = sb("gg", [P, 2], F32, late)
        o_s = sb("o_s", [P, P], F32, late)
        pages = sb("pages", [1, NS * NP], I32, late)
        q_all = sb("q_all", [P, 2, P], F32, late)
        few = sb("few", [P, 24], F32, late)
        krq_s = sb("krq_s", [P, NS], F32, late)[:, :]
        inv_sum = sb("inv_sum", [P, QB], F32, late)[:, :]
        proj = ExitStack()
        trig = sb("trig", [P, 2, TOK], F32, proj)
        cq = sb("cq", [P, 2, TOK], F32, proj)
        trig_g = sb("trig_g", [P, 2, TOK], F32, proj)
        tq = sb("tq", [P, 2, TOK], F32, proj)
        rope_a = sb("rope_a", [P, TOK], F32, proj)
        rope_b = sb("rope_b", [P, TOK], F32, proj)
        sq_h = sb("sq_h", [P, 2, TOK], F32, proj)
        kr_raw = rope_a[:, :]
        wuk_t = sb("wuk_t", [P, 2, P], F32, proj)
        proj.close()
        at_h, at_w = 2 * SLOT, 2 * SLOT + 2 * KC * TOK
        starts = [(at_h + 2 * TOK, 3), (at_h + (KC + 2) * TOK, 3),
                  (at_w, 4), (at_w + 2 * SLOT, 4), (SLOT, 2)]
        pieces = [over[:, s + i * 4 * CD:s + (i + 1) * 4 * CD].rearrange("p (j c) -> p j c", j=4)
                  for s, n in starts for i in range(n)]
        kt = raw[:, 0, :].rearrange("p (a b c) -> p a b c", a=2, b=2)
        order = [(2 * (i // 4) + i % 2, i % 4 // 2) for i in range(2 * NS)]
        sd = raw[:, 0, 0:PAST + NS]
        ks_all = square[:, :, :].rearrange("p a n -> p (a n)")[:, 0:NP * P].rearrange("p (j c) -> p j c", j=NP)
        ks_new = square_sum[0:NS, 0:2 * P].rearrange("p (a c) -> p a c", a=2)
        p_new = square_sum[0:NS, 2 * P:3 * P]
        o_rows = raw[0:H, 0, 0:NS * KL].rearrange("p (b c) -> p b c", b=NS)
        s_new = square_sum[:, 3 * P:3 * P + NS]
        heads = ExitStack()
        scores_at = ExitStack()
        q_pad = sb("q_pad", [P, 2, NS, P], F32, scores_at)
        scores_at.close()
        prob = sb("prob", [P, 10 * P], F32, heads)
        prob_t = sb("prob_t", [P, 10 * P], F32, heads)
        cks = sb("cks", [P, 2, SEQ], F32, heads)
        krs = sb("krs", [P, 2, SEQ], F32, heads)
        o_t = sb("o_t", [P, TOK], F32, heads)
        heads.close()
        late.close()

        main = ctx.enter_context(nc.psum_tensor("main", [P, 2, 2, 512], F32))
        side = ctx.enter_context(nc.psum_tensor("side", [P, 4, 512], F32))

        const_in = sem("const_in")
        x_in = [sem("x_in0"), sem("x_in1")]
        vectors_in = sem("vectors_in")
        vectors_turned = sem("vectors_turned")
        vectors_set = sem("vectors_set")
        ws_in = sem("ws_in")
        raw_in = [sem("raw_in0"), sem("raw_in1")]
        hi_done = sem("hi_done")
        lo_done = sem("lo_done")
        tile_done = sem("tile_done")
        evac_done = sem("evac_done")
        act_done = sem("act_done")
        mul_done = sem("mul_done")
        h_hi_done = sem("h_hi_done")
        h_lo_done = sem("h_lo_done")
        xg_hi_done = sem("xg_hi_done")
        xg_lo_done = sem("xg_lo_done")
        square_done = sem("square_done")
        sum_done = sem("sum_done")
        rms_mm = sem("rms_mm")
        root_done = sem("root_done")
        rstd_done = sem("rstd_done")
        eps_set = sem("eps_set")
        out_turned = sem("out_turned")
        out_copied = sem("out_copied")
        out_written = sem("out_written")
        ws_masked = sem("ws_masked")
        ws_turned = sem("ws_turned")
        ws_copied = sem("ws_copied")
        vg_done = sem("vg_done")
        v_turned = sem("v_turned")
        v_copied = sem("v_copied")
        vs_out = [sem("vs_out0"), sem("vs_out1")]
        mix_done = sem("mix_done")
        mixed = sem("mixed")
        v_seen = sem("v_seen")
        sample_mix = sem("sample_mix")

        kv_in = sem("kv_in")
        pages_in = sem("pages_in")
        nat_in = [sem(f"nat_in{b}") for b in range(NS)]
        gg_set = sem("gg_set")
        trig_set = sem("trig_set")
        cq_squared = sem("cq_squared")
        cqn_set = sem("cqn_set")
        c_squared = sem("c_squared")
        c_set = sem("c_set")
        kr_swapped = sem("kr_swapped")
        kr_part = sem("kr_part")
        kr_set = sem("kr_set")
        rope_part = sem("rope_part")
        row_turned = sem("row_turned")
        row_copied = sem("row_copied")
        rows_done = sem("rows_done")
        tq_read = sem("tq_read")
        q_ssq = sem("q_ssq")
        swapped = sem("swapped")
        rope_b_set = sem("rope_b_set")
        rope_a_set = sem("rope_a_set")
        qr_set = sem("qr_set")
        q_ssq_read = sem("q_ssq_read")
        wuk_turned = sem("wuk_turned")
        wuk_copied = sem("wuk_copied")
        kn_done = sem("kn_done")
        kn_squared = sem("kn_squared")
        k_ssq = sem("k_ssq")
        lat_done = sem("lat_done")
        lat_copied = sem("lat_copied")
        kr_squared = sem("kr_squared")
        ssq_set = sem("ssq_set")
        ssq_root = sem("ssq_root")
        scale_set = sem("scale_set")
        q_all_set = sem("q_all_set")
        ks_all_set = sem("ks_all_set")
        nat_turned = sem("nat_turned")
        kt_c_copied = sem("kt_c_copied")
        kt_r_copied = sem("kt_r_copied")
        nat_used = sem("nat_used")
        ks_turned = sem("ks_turned")
        ks_copied = sem("ks_copied")
        qpad_zero = sem("qpad_zero")
        q_pad_set = sem("q_pad_set")
        pv_summed = sem("pv_summed")
        o_rows_set = sem("o_rows_set")
        new_scored = sem("new_scored")
        ks_new_set = sem("ks_new_set")
        new_ready = sem("new_ready")
        sd_set = sem("sd_set")
        sd_max = sem("sd_max")
        sd_exp = sem("sd_exp")
        sd_inv = sem("sd_inv")
        sd_prob = sem("sd_prob")
        sd_turned = sem("sd_turned")
        sd_t_copied = sem("sd_t_copied")
        os_done = sem("os_done")
        os_copied = sem("os_copied")
        ks_rows_turned = sem("ks_rows_turned")
        ks_hi_set = sem("ks_hi_set")
        ks_lo_set = sem("ks_lo_set")
        scales_spread = sem("scales_spread")
        c_scaled = sem("c_scaled")
        kr_scaled = sem("kr_scaled")
        scored = sem("scored")
        max_set = sem("max_set")
        max_done = sem("max_done")
        exp_done = sem("exp_done")
        inv_done = sem("inv_done")
        prob_done = sem("prob_done")
        prob_turned = sem("prob_turned")
        prob_t_act = sem("prob_t_act")
        prob_t_dve = sem("prob_t_dve")
        pv_done = sem("pv_done")
        o_copied = sem("o_copied")
        o_samples = sem("o_samples")
        uv_done = sem("uv_done")
        uv_copied = sem("uv_copied")
        tq_squared = sem("tq_squared")
        dkv_rope_in = sem("dkv_rope_in")
        uq_rope_in = [sem("uq_rope_in0"), sem("uq_rope_in1")]

        at_ffn = [None] * 4
        at_ffn[0] = At(tile=KD, evac=KD, sums=KD)
        at_gmlp = ffn_past(at_ffn[0])
        THIRD = -(-(SLOT // 2 + 4 * QK) // 3)
        n_v, n_u, n_out = GT // 2, GT // 2, 8
        gmlp_chunks = n_v + n_u + n_out
        at_ffn[1] = at_gmlp.past(gmlp_chunks, 2 * gmlp_chunks, 2 * gmlp_chunks, GT, GT, 2 * GT, 1, 2, GT + KD)
        at_ffn[2] = ffn_past(at_ffn[1])
        at_mla = ffn_past(at_ffn[2])
        at_uq = at_mla.past(chunk=2, tile=4, evac=4, h=2, rms=3)
        at_wo = at_uq.past(chunk=4, tile=24, evac=24)
        at_ffn[3] = at_wo.past(chunk=8, tile=16, evac=16, h=H, norm=1, sums=KD)
        P_AT = [0, 1, 3, 6]
        PT_AT = [0, 4, 8, 7]
        at_end = ffn_past(at_ffn[3], last=True)
        last_chunk = at_end.chunk - 1
        norm_of = [(0, 0), (0, 1), (0, 2), (1, 0), (1, 1), (1, 2)]

        def w_rows(w):
            return w.rearrange("(k p) n -> p k n", p=P)

        def vector_sources():
            out, row0 = [], 0
            for src, n in ((norm_g.rearrange("i j (k p) -> (i j k) p", p=P), n_gain),
                           (gmlp_b_in[0].rearrange("(k p) -> k p", p=P), n_bias),
                           (gmlp_v_norm[0].rearrange("(k p) -> k p", p=P), n_vg),
                           (mla_q_norm[0].rearrange("(k p) -> k p", p=P), 2), (mla_kv_norm, 1),
                           (mla_qk_gain_q[:, 0:NOPE], 1), (mla_qk_gain_k[:, 0:NOPE], 1)):
                out.append((vector_rows[row0:row0 + n, :], src))
                row0 += n
            for src in (mla_qk_gain_q, mla_qk_gain_k):
                for a in range(2):
                    out.append((vector_rows[row0:row0 + 1, a * ROPE:(a + 1) * ROPE], src[:, NOPE:QK]))
                row0 += 1
            return out

        block = ctx.enter_context(nc.Block())

        @block.sync
        def _(sp):
            x_rows = x_prompt[0].rearrange("(q p) d -> p q d", p=P)
            sp.dma_start(x_tok[:, :, 0:D // 2], x_rows[:, :, 0:D // 2]).then_inc(x_in[0], 16)
            small = vector_sources()
            for dst, src in small[:6]:
                sp.dma_start(dst, src).then_inc(vectors_in, 16)
            sp.dma_start(x_tok[:, :, D // 2:D], x_rows[:, :, D // 2:D]).then_inc(x_in[1], 16)

            def load(n, slot, w, k0, nk, c0, nc_=WC):
                if not isinstance(n, int) or n >= 2:
                    sp.wait_ge(lo_done, n - 1)
                dst = raw[:, slot, :].rearrange("p (k c) -> p k c", k=KC)[:, 0:nk, 0:nc_]
                cols = slice(c0, c0 + nc_) if isinstance(c0, int) else bass.ds(c0, nc_)
                sp.dma_start(dst, w_rows(w)[:, k0:k0 + nk, cols]).then_inc(raw_in[slot], 16)

            def ffn(at, layer, which):
                wg, wu, wd = ffn_w_gate[layer, which], ffn_w_up[layer, which], ffn_w_down[layer, which]
                n, f0 = at.chunk, 0
                for pairs in FF_GROUPS:
                    def gate_up(i, n=n, f0=f0):
                        load(n + 2 * i, 0, wg, 0, KD, (f0 + i) * WC)
                        load(n + 2 * i + 1, 1, wu, 0, KD, (f0 + i) * WC)
                    start = 1 if n < 2 else 0
                    if start:
                        gate_up(0)
                    with sp.Fori(0, pairs - start) as i:
                        gate_up(i + start)
                    n += 2 * pairs

                    with sp.Fori(0, 2) as i:
                        for s in range(2):
                            load(n + 2 * i + s, s, wd, 2 * f0, 2 * pairs, (2 * i + s) * WC)
                    n += 4
                    f0 += pairs

            ffn(at_ffn[0], 0, 0)
            n = at_gmlp.chunk
            with sp.Fori(0, n_v // 2) as i:
                for s in range(2):
                    load(n + 2 * i + s, s, gmlp_w_in[0], 0, KD, (2 * i + s) * WC + GM)
            n += n_v
            for q in range(2):
                with sp.Fori(0, n_u // 4) as i:
                    for s in range(2):
                        load(n + 2 * i + s, s, gmlp_w_in[0], 0, KD, (2 * i + s) * WC + q * GM // 2)
                n += n_u // 2
                with sp.Fori(0, 2) as i:
                    for s in range(2):
                        load(n + 2 * i + s, s, gmlp_w_out[0], q * KC, KC, (2 * i + s) * WC)
                n += 4
            ffn(at_ffn[1], 0, 1)
            ffn(at_ffn[2], 1, 0)

            n = at_mla.chunk
            load(n, 0, mla_w_dq[0], 0, KD, 0)
            sp.wait_ge(lo_done, n)
            dst = raw[:, 1, :].rearrange("p (k c) -> p k c", k=KC)
            sp.dma_start(dst[:, :, 0:KL + ROPE], w_rows(mla_w_dkv[0])).then_inc(raw_in[1], 16)
            sp.dma_start(dst[:, :, KL + ROPE:KL + 2 * ROPE], w_rows(mla_w_dkv[0])[:, :, KL:KL + ROPE]).then_inc(dkv_rope_in, 16)
            sp.dma_start(wkv[:], mla_w_uk[0]).then_inc(kv_in, 16)
            sp.wait_ge(h_lo_done, at_mla.h)
            sp.dma_start(trig[:].rearrange("p a n -> p (a n)"), table[:, N_CONST:N_CONST + N_TRIG]).then_inc(kv_in, 16)
            sp.dma_start(pages[:], page_table.rearrange("b n -> (b n)").unsqueeze(0)).then_inc(pages_in, 16)

            def load_pages(first, last):
                for k in range(first, last):
                    for j in range(4):
                        page = sp.value_load(pages[0:1, 4 * k + j:4 * k + j + 1], min_val=0, max_val=POOL - 1)
                        sp.dma_start(pieces[k][:, j, :], cache_mla[0, bass.ds(page, 1), :, :].rearrange("a p d -> (a p) d"))\
                            .then_inc(nat_in[k // 2], 16)

            n = at_uq.chunk
            for c in range(4):
                if c == 2:
                    sp.wait_ge(pages_in, 16)
                    sp.wait_ge(tile_done, at_mla.tile)
                    load_pages(0, 6)
                sp.wait_ge(lo_done, n + c - 1)
                src = mla_w_uq[0].rearrange("(k p) h d -> k p h d", p=P)[:, :, 4 * c:4 * c + 4, :]
                for k in range(2):
                    dst = raw[:, c % 2, k * 1024:k * 1024 + 4 * QK]
                    sp.dma_start(dst[:, 4 * NOPE:].rearrange("p (h d) -> p h d", h=4), src[k, :, :, NOPE:QK])\
                        .then_inc(uq_rope_in[c % 2], 16)
                    sp.dma_start(dst[:, 0:4 * NOPE].rearrange("p (h d) -> p h d", h=4), src[k, :, :, 0:NOPE])\
                        .then_inc(uq_rope_in[c % 2] if k else raw_in[c % 2], 16)
            sp.wait_ge(tile_done, at_wo.tile)
            sp.wait_ge(lo_done, at_wo.chunk)
            load_pages(6, 2 * NS)
            sp.wait_ge(lat_done, H)
            sp.dma_start(wkv[:], mla_w_uv[0]).then_inc(kv_in, 16)
            sp.wait_ge(rows_done, 1)
            sp.dma_start(new_prompt[0, 0].rearrange("(q p) d -> p q d", p=P), rows[:]).then_inc(out_written, 16)
            sp.dma_start(new_sample[0, :, 0, :], rows_s[:]).then_inc(out_written, 16)
            sp.wait_ge(os_done, 1)
            n = at_wo.chunk
            for q in range(2):
                for c in range(4):
                    load(n, c % 2, mla_w_o[0], q * KC, KC, c * WC)
                    n += 1
            ffn(at_ffn[3], 1, 1)
            sp.wait_ge(out_copied, KD)
            yt = x_tok
            sp.dma_start(y_prompt[0].rearrange("(q p) d -> p q d", p=P), yt).then_inc(out_written, 16)
            sp.dma_start(y_sample[:, 0, :], xs_tok).then_inc(out_written, 16)
            sp.wait_ge(out_written, 64)

        @block.tensor
        def _(pe):
            def out_tile(m, slot, k_tiles, hi, lo, before=None, free=None):
                if free is not None:
                    pe.wait_ge(evac_done, free)
                ws = [w[:, slot, :].rearrange("p (k c) -> p k c", k=KC) for w in (w_hi, w_lo)]
                for k in range(k_tiles):
                    if before and k in before:
                        before[k]()
                    for n, (w, moving) in enumerate(((ws[0], hi), (ws[0], lo), (ws[1], hi))):
                        for half in range(2):
                            mm = nc.tensor.matmul(main[:, m, half, 0:HALF], w[:, k, m * P:(m + 1) * P],
                                                  moving[:, k, half * HALF:(half + 1) * HALF],
                                                  start=(k == 0 and n == 0), stop=(k == k_tiles - 1 and n == 2))
                mm.then_inc(tile_done, 1)

            def rms(at):
                def go():
                    pe.wait_ge(sum_done, at.sums)
                    for half in range(2):
                        mm = nc.tensor.matmul(side[:, half, 0:HALF], ones, square_sum[:, half * HALF:(half + 1) * HALF],
                                              start=True, stop=True)
                    mm.then_inc(rms_mm, 1)
                return go

            def down(n, e, h, k_tiles, m_tiles=2, slot=0):
                pe.wait_ge(lo_done, n + 1)
                for m in range(2):
                    before = {}
                    if m == 0:
                        pe.wait_ge(h_lo_done, h + k_tiles - 2)
                        before[k_tiles - 2] = lambda: pe.wait_ge(h_lo_done, h + k_tiles)
                    out_tile(m, slot, k_tiles, h_hi, h_lo, before=before, free=e + m - 1)

            def ffn(at, final):
                n, e, h = at.chunk, at.evac, at.h
                for g, pairs in enumerate(FF_GROUPS):
                    def gate_up(i, n=n, e=e, rms_at=None):
                        for s in range(2):
                            pe.wait_ge(lo_done, n + 2 * i + s + 1)
                            for m in range(2):
                                before = {4: rms_at} if rms_at and s == 0 and m == 0 else {}
                                if rms_at and s == 0 and m == 0:
                                    pe.wait_ge(xg_lo_done, KD * at.norm + KD - 2)
                                    before[KD - 2] = lambda: pe.wait_ge(xg_lo_done, KD * at.norm + KD)
                                out_tile(m, s, KD, xg_hi, xg_lo, before=before, free=e + 4 * i + 2 * s + m - 1)
                    start = 0
                    if g == 0:
                        gate_up(0, rms_at=rms(at))
                        start = 1
                    with pe.Fori(0, pairs - start) as i:
                        gate_up(i + start)
                    n, e, h = n + 2 * pairs, e + 4 * pairs, h + 2 * pairs
                    if g + 1 < len(FF_GROUPS):
                        with pe.Fori(0, 2) as i:
                            for s in range(2):
                                down(n + 2 * i + s, e + 4 * i + 2 * s, h - 2 * pairs, 2 * pairs, slot=s)
                    else:
                        for i in range(4):
                            down(n + i, e + 2 * i, h - 2 * pairs, 2 * pairs, slot=i % 2)
                    n, e = n + 4, e + 8

            pe.wait_ge(const_in, 16 * 2)
            pe.wait_ge(vectors_in, 16 * 11)
            nc.tensor.transpose(side[:, 0, 0:n_vec], vector_rows[0:n_vec, :], ident[0:n_vec, 0:n_vec]).then_inc(vectors_turned, 1)
            for k in range(KD):
                if k % (KD // 2) == 0:
                    pe.wait_ge(x_in[k // (KD // 2)], 16)
                if k >= 2:
                    pe.wait_ge(evac_done, k - 1)
                for q in range(QB):
                    nc.tensor.transpose(main[:, k % 2, 0, q * P:(q + 1) * P], x_tok[:, q, k * P:(k + 1) * P], ident)
                nc.tensor.transpose(main[:, k % 2, 1, 0:NS], xs_tok[:, k * P:(k + 1) * P],
                                    ident[0:NS, 0:NS]).then_inc(tile_done, 1)
            ffn(at_ffn[0], False)

            n, e = at_gmlp.chunk, at_gmlp.evac

            def v_chunk(i, s, first=False):
                pe.wait_ge(lo_done, n + 2 * i + s + 1)
                for m in range(2):
                    before = {}
                    if first and m == 0:
                        pe.wait_ge(xg_lo_done, KD * at_gmlp.norm + KD - 2)
                        before = {4: rms(at_gmlp), KD - 2: lambda: pe.wait_ge(xg_lo_done, KD * at_gmlp.norm + KD)}
                    out_tile(m, s, KD, xg_hi, xg_lo, before=before, free=e + 4 * i + 2 * s + m - 1)
            v_chunk(0, 0, True)
            pe.wait_ge(ws_masked, 1)
            for g in range(NG):
                t = nc.tensor.transpose(side[:, 2 + g // 4, (g % 4) * P:(g % 4 + 1) * P], ws_nat[:, g, :], ident)
            t.then_inc(ws_turned, 1)
            v_chunk(0, 1)
            with pe.Fori(0, n_v // 2 - 1) as i:
                v_chunk(i + 1, 0)
                v_chunk(i + 1, 1)
            n, e = n + n_v, e + 2 * n_v

            def rms_v():
                pe.wait_ge(sum_done, at_gmlp.sums + GT)
                pe.wait_ge(ws_copied, 1)
                for q in range(QB):
                    nc.tensor.matmul(side[:, 2, q:q + 1], square_sum[:, q * P:(q + 1) * P], ones[:, 0:1],
                                     start=True, stop=True)
                nc.tensor.matmul(side[:, 2, QB:QB + NS], ones, square_sum[:, SEQ:TOK], start=True, stop=True)
                nc.tensor.matmul(side[0:NS, 2, QB + NS:QB + NS + 1], square_sum[:, SEQ:TOK], ones[:, 0:1],
                                 start=True, stop=True).then_inc(rms_mm, 1)

            for g in range(NG):
                if g == NG // 2:
                    for i in range(2):
                        for s in range(2):
                            down(n, e, at_gmlp.h, KC, slot=s)
                            n, e = n + 1, e + 2
                pe.wait_ge(lo_done, n + 1)
                out_tile(0, g % 2, KD, xg_hi, xg_lo, before={4: rms_v} if g == 0 else {}, free=e - 1)
                pe.wait_ge(vg_done, 2 * g + 2)
                if g == 0:
                    pe.wait_ge(root_done, at_gmlp.rms + 2)
                else:
                    pe.wait_ge(mixed, 2 * g)
                    pe.wait_ge(v_seen, g)
                for m in range(2):
                    for q in range(QB):
                        nc.tensor.transpose(side[:, m, q * P:(q + 1) * P], v[:, 2 * g + m, q * P:(q + 1) * P], ident)
                    t = nc.tensor.transpose(side[0:NS, 2, m * P:(m + 1) * P], v[:, 2 * g + m, SEQ:TOK], ident)
                t.then_inc(v_turned, 1)
                out_tile(1, g % 2, KD, xg_hi, xg_lo, free=e)
                for m in range(2):
                    pe.wait_ge(v_copied, 2 * g + m + 1)
                    pe.wait_ge(ws_copied, 1)
                    bank = (3, 0)[m]
                    for q in range(QB):
                        mm = nc.tensor.matmul(side[:, bank, q * P:(q + 1) * P], v_tok[:, m, q, :], ws_t[:, g, :],
                                              start=True, stop=True)
                    mm.then_inc(mix_done, 1)
                n, e = n + 1, e + 2
            for i in range(4):
                down(n, e, at_gmlp.h + KC, KC, slot=i % 2)
                n, e = n + 1, e + 2
            ffn(at_ffn[1], False)
            ffn(at_ffn[2], False)

            n, e = at_mla.chunk, at_mla.evac
            pe.wait_ge(xg_lo_done, KD * at_mla.norm + KD - 2)
            pe.wait_ge(lo_done, n + 1)
            out_tile(0, 0, KD, xg_hi, xg_lo, free=e - 1,
                     before={4: rms(at_mla), KD - 2: lambda: pe.wait_ge(xg_lo_done, KD * at_mla.norm + KD)})
            out_tile(1, 0, KD, xg_hi, xg_lo, free=e)
            pe.wait_ge(lo_done, n + 2)
            out_tile(0, 1, KD, xg_hi, xg_lo, free=e + 1)

            def wide_sum(bank, stationary, moving, parts=1):
                for half in range(2):
                    for i in range(parts):
                        mm = nc.tensor.matmul(side[:, bank + half, 0:HALF], stationary,
                                              moving[i][:, half * HALF:(half + 1) * HALF],
                                              start=(i == 0), stop=(i == parts - 1))
                return mm

            pe.wait_ge(cq_squared, 2)
            pe.wait_ge(root_done, at_mla.rms + 1)
            wide_sum(0, ones, [square[:, 0, :], square[:, 1, :]], 2).then_inc(rms_mm, 1)
            out_tile(1, 1, KD, xg_hi, xg_lo, free=e + 2)
            pe.wait_ge(c_squared, 1)
            wide_sum(2, ones, [tq[:, 0, :]]).then_inc(rms_mm, 1)
            pe.wait_ge(evac_done, e + 4)
            pe.wait_ge(root_done, at_mla.rms + 2)
            wide_sum(0, swap, [kr_raw]).then_inc(kr_swapped, 1)

            n, e = at_uq.chunk, at_uq.evac
            pe.wait_ge(h_lo_done, at_uq.h)

            def q_after(u):
                c, part = u // 6, u % 6
                rope = part % 3 == 2
                if rope:
                    r_ = 2 * c + part // 3
                    pe.wait_ge(rope_b_set, r_ + 1)
                    pe.wait_ge(evac_done, e + u + 1)
                    wide_sum(0, swap, [tq[:, u % 2, :]]).then_inc(swapped, 1)
                pe.wait_ge(tq_squared, u + 1)
                h0 = 4 * c + 2 * (part // 3)
                base, hh, w = (5 * H, h0, 2) if rope else (0, h0 + part % 3, 1)
                rhs = two if rope else ones[:, 0:1]
                for b in range(QB + 1):
                    rows_ = P if b < QB else NS
                    mm = nc.tensor.matmul(side[0:rows_, 2, base + b * H + hh:base + b * H + hh + w],
                                          sq_h[:, u % 2, b * P:b * P + rows_], rhs, start=True, stop=True)
                mm.then_inc(q_ssq, 1)

            pe.wait_ge(root_done, at_uq.rms)
            for u in range(24):
                c, part = u // 6, u % 6
                if part == 0:
                    pe.wait_ge(lo_done, n + c + 1)
                pe.wait_ge(evac_done, e + u - 1)
                h0 = 2 * (part // 3)
                for k in range(2):
                    for i, (w, moving) in enumerate(((w_hi, h_hi), (w_hi, h_lo), (w_lo, h_hi))):
                        col = k * 1024 + (4 * NOPE + h0 * ROPE if part % 3 == 2 else (h0 + part % 3) * NOPE)
                        st = w[:, c % 2, col:col + P]
                        for half in range(2):
                            mm = nc.tensor.matmul(main[:, u % 2, half, 0:HALF], st,
                                                  moving[:, k, half * HALF:(half + 1) * HALF],
                                                  start=(k == 0 and i == 0), stop=(k == 1 and i == 2))
                mm.then_inc(tile_done, 1)
                if u > 0:
                    q_after(u - 1)
            q_after(23)

            pe.wait_ge(rope_b_set, 9)
            pe.wait_ge(evac_done, at_wo.evac)
            for b in range(QB + 1):
                w = P if b < QB else NS
                if b == 0:
                    pe.wait_ge(c_set, 1)
                    pe.wait_ge(kr_set, 1)
                if b >= 2:
                    pe.wait_ge(row_copied, b - 1)
                nc.tensor.transpose(side[0:w, b % 2, 0:P], c_t[:, b * P:b * P + w], ident)
                nc.tensor.transpose(side[0:w, b % 2, P:2 * P], kr_t[:, b * P:b * P + w], ident).then_inc(row_turned, 1)
            pe.wait_ge(kv_in, 32)
            pe.wait_ge(kr_squared, 1)
            for b in range(QB + 1):
                w = P if b < QB else NS
                nc.tensor.matmul(side[0:w, 3, 5 * H + b:5 * H + b + 1], sq_h[0:ROPE, 0, b * P:b * P + w],
                                 ones[0:ROPE, 0:1], start=True, stop=True)

            def k_norms(h):
                pe.wait_ge(kn_squared, h + 1)
                for b in range(QB + 1):
                    w = P if b < QB else NS
                    mm = nc.tensor.matmul(side[0:w, 3, b * H + h:b * H + h + 1], sq_h[:, h % 2, b * P:b * P + w],
                                          ones[:, 0:1], start=True, stop=True)
                mm.then_inc(k_ssq, 1)

            for h in range(H):
                if h == 0:
                    pe.wait_ge(row_copied, QB + 1)
                if h >= 2:
                    pe.wait_ge(wuk_copied, h - 1)
                nc.tensor.transpose(side[:, h % 2, 0:P], wkv[:, h, :], ident).then_inc(wuk_turned, 1)
                if h >= 1:
                    pe.wait_ge(kn_squared, h)
                for half in range(2):
                    mm = nc.tensor.matmul(main[:, 0, half, 0:HALF], wkv[:, h, :], c_t[:, half * HALF:(half + 1) * HALF],
                                          start=True, stop=True)
                mm.then_inc(kn_done, 1)
                if h >= 1:
                    k_norms(h - 1)
                    pe.wait_ge(lat_copied, h)
                pe.wait_ge(wuk_copied, h + 1)
                pe.wait_ge(tq_read, 24)
                for half in range(2):
                    mm = nc.tensor.matmul(main[:, 1, half, 0:HALF], wuk_t[:, h % 2, :],
                                          qn[:, h, half * HALF:(half + 1) * HALF], start=True, stop=True)
                mm.then_inc(lat_done, 1)
            k_norms(H - 1)

            pe.wait_ge(ssq_set, 2)

            def turn_keys(k):
                b, half = order[k]
                keys = pieces[2 * b + half]
                if half == 0:
                    pe.wait_ge(nat_in[b], 128)
                if k >= 2:
                    pe.wait_ge(kt_c_copied, k - 1)
                    pe.wait_ge(kt_r_copied, k - 1)
                for j in range(4):
                    t = nc.tensor.transpose(side[:, 2 * (k % 2), j * P:(j + 1) * P], keys[:, j, 0:KL], ident)
                t.then_inc(nat_turned, 1)
                for j in range(4):
                    t = nc.tensor.transpose(side[0:ROPE, 2 * (k % 2) + 1, j * P:(j + 1) * P],
                                            keys[:, j, KL:KL + ROPE], ident)
                t.then_inc(nat_turned, 1)

            def spread_scales(h, bank=side[:, 0, :]):
                for part in (ks_hi, ks_lo):
                    mm = nc.tensor.matmul(bank, pick[:, h:h + 1].to_broadcast([H, P]), part[:],
                                          start=(part is ks_hi), stop=(part is ks_lo))
                mm.then_inc(scales_spread, 1)

            turn_keys(0)
            pe.wait_ge(lat_copied, H)
            pe.wait_ge(rows_done, 1)
            for b in range(QB):
                t = nc.tensor.transpose(main[0:H, 1, 1, b * P:(b + 1) * P], rows[:, b, KL + ROPE:CD], ident)
            t.then_inc(ks_rows_turned, 1)
            pe.wait_ge(lat_copied, H)
            pe.wait_ge(q_all_set, 3)
            nc.tensor.matmul(main[:, 1, 0, 0:NS], q_all[:, 0, :], c_t[:, SEQ:TOK], start=True, stop=False)
            nc.tensor.matmul(main[:, 1, 0, 0:NS], q_all[0:ROPE, 1, :], kr_t[0:ROPE, SEQ:TOK], start=False, stop=True)
            pe.wait_ge(ks_new_set, 2)
            nc.tensor.matmul(main[:, 1, 0, NS:2 * NS], ks_new[:, 0, :], ident[0:NS, 0:NS], start=True, stop=True)
            nc.tensor.matmul(main[:, 1, 0, 2 * NS:2 * NS + 1], ks_new[:, 1, :], ones[0:NS, 0:1], start=True,
                             stop=True).then_inc(new_scored, 1)
            for k in range(2 * NS):
                if k + 1 < 2 * NS:
                    turn_keys(k + 1)
                b, half = order[k]
                pe.wait_ge(kt_c_copied, k + 1)
                if k == 0:
                    pe.wait_ge(q_pad_set, 1)
                mm = nc.tensor.matmul(main[:, 0, half, :], q_pad[:, 0, b, :], kt[:, k % 2, 0, :], start=(b == 0), stop=False)
                if k % 2 == 1:
                    pe.wait_ge(kt_r_copied, k + 1)
                    mm = nc.tensor.matmul(main[:, 0, half, :], q_pad[:, 1, b // 2, :], kt[:, k // 2 % 2, 1, :], start=False,
                                          stop=(b == NS - 1))
                mm.then_inc(nat_used, 1)
                if k == NS // 2:
                    pe.wait_ge(new_ready, 2)
                    pe.wait_ge(ks_lo_set, 1)
                    spread_scales(0, main[:, 1, 0, :])
                if k == 2 * NS - 4:
                    pe.wait_ge(kr_scaled, 1)
                    pe.wait_ge(ks_all_set, 1)
                    for j in range(NP):
                        t = nc.tensor.transpose(main[:, 1, j // 4, (j % 4) * P:(j % 4 + 1) * P], ks_all[:, j, :], ident)
                    t.then_inc(ks_turned, 1)
            pe.wait_ge(kt_c_copied, 2 * NS)
            pe.wait_ge(kt_r_copied, 2 * NS)

            def scores(h):
                pe.wait_ge(c_scaled, h + 1)
                pe.wait_ge(kr_scaled, h + 1)
                lo = ROPE * (h % 2)
                for q in range(QB):
                    if h >= 1:
                        pe.wait_ge(exp_done, QB * (h - 1) + q + 1)
                    bank = main[:, q // 2, q % 2, :]
                    nk = (q + 1) * P
                    nc.tensor.matmul(bank[:, 0:nk], qn[:, h, q * P:(q + 1) * P], cks[:, h % 2, 0:nk], start=True, stop=False)
                    nc.tensor.matmul(bank[:, 0:nk], qr[lo:lo + ROPE, h // 2, q * P:(q + 1) * P],
                                     krs[lo:lo + ROPE, h % 2, 0:nk], start=False, stop=False)
                    mm = nc.tensor.matmul(bank[:, q * P:nk], mask_ops[:, 0, :], mask_ops[:, 1, :], start=False, stop=True)
                mm.then_inc(scored, 1)

            pe.wait_ge(sd_set, 2)
            pe.wait_ge(ks_copied, 1)
            scores(0)
            spread_scales(1)
            pe.wait_ge(sd_prob, 1)
            for j in range(NP):
                nc.tensor.transpose(side[:, 2 + j // 4, (j % 4) * P:(j % 4 + 1) * P], sd[:, j * P:(j + 1) * P], ident)
            nc.tensor.transpose(side[0:NS, 1, 0:P], sd[:, PAST:PAST + NS], ident).then_inc(sd_turned, 1)
            pe.wait_ge(sd_t_copied, 2)
            pe.wait_ge(rows_done, 1)
            for k in range(2 * NS):
                b = k // 2
                for j in range(4):
                    blk = 4 * (k % 2) + j
                    nc.tensor.matmul(side[0:H, 2 + b // 4, (b % 4) * P:(b % 4 + 1) * P], ks_all[:, blk, b * H:(b + 1) * H],
                                     pieces[k][:, j, 0:KL], start=(blk == 0), stop=False)
                if k % 2 == 1:
                    mm = nc.tensor.matmul(side[0:H, 2 + b // 4, (b % 4) * P:(b % 4 + 1) * P], p_new[:, b * H:(b + 1) * H],
                                          rows_s[:, 0:KL], start=False, stop=True)
            mm.then_inc(pv_summed, 1)
            pe.wait_ge(o_rows_set, 1)
            for b in range(NS):
                t = nc.tensor.transpose(side[:, 1, b * H:(b + 1) * H], o_rows[:, b, :], ident[0:H, 0:H])
            t.then_inc(os_done, 1)

            pe.wait_ge(os_copied, 1)
            pe.wait_ge(kv_in, 48)

            def turn(h, blocks, bank):
                at = 0
                for k in blocks:
                    for q in range(k, QB):
                        t = nc.tensor.transpose(side[:, bank, at * P:(at + 1) * P],
                                                prob[:, (P_AT[q] + k) * P:(P_AT[q] + k + 1) * P], ident)
                        at += 1
                t.then_inc(prob_turned, 1)

            n, e = at_wo.chunk, at_wo.evac
            for h in range(H + 1):
                if 0 < h < H:
                    scores(h)
                g = h - 1
                if g >= 0:
                    pe.wait_ge(prob_done, g + 1)
                    if g >= 1:
                        pe.wait_ge(o_copied, g)
                        pe.wait_ge(uv_copied, g)
                    turn(g, (0,), 2)
                    turn(g, (1, 3), 3)
                    turn(g, (2,), 1)
                if 0 < h < H - 1:
                    spread_scales(h + 1)
                if g >= 0:
                    for k, copied, count in ((0, prob_t_act, 2 * g + 1), (1, prob_t_dve, g + 1), (3, prob_t_dve, g + 1),
                                             (2, prob_t_act, 2 * g + 2)):
                        pe.wait_ge(copied, count)
                        mm = nc.tensor.matmul(side[:, 2, k * P:SEQ], rows[:, k, 0:KL],
                                              prob_t[:, PT_AT[k] * P:(PT_AT[k] + QB - k) * P], start=(k == 0),
                                              stop=(k == 2))
                    mm.then_inc(pv_done, 1)
                if g >= 0:
                    pe.wait_ge(o_copied, g + 1)
                    pe.wait_ge(o_samples, g + 1)
                    nc.tensor.matmul(side[:, 3, 0:SEQ], wkv[:, g, :], o_t[:, 0:SEQ], start=True, stop=True)
                    nc.tensor.matmul(side[:, 1, 0:NS], wkv[:, g, :], o_t[:, SEQ:TOK], start=True,
                                     stop=True).then_inc(uv_done, 1)
                if g == KC - 1 or g == H - 1:
                    pe.wait_ge(exp_done, QB * min(h + 1, H))
                    for i in range(4):
                        down(n, e, at_wo.h + h - KC, KC, slot=i % 2)
                        n, e = n + 1, e + 2
                    pe.wait_ge(evac_done, e)
            ffn(at_ffn[3], True)
            for k in range(KD):
                pe.wait_ge(evac_done, at_end.evac - KD + k + 1)
                if k >= 2:
                    pe.wait_ge(out_copied, k - 1)
                for q in range(QB):
                    nc.tensor.transpose(side[:, k % 2, q * P:(q + 1) * P], x[:, k, q * P:(q + 1) * P], ident)
                nc.tensor.transpose(side[0:NS, 2 + k % 2, 0:P], x[:, k, SEQ:TOK], ident).then_inc(out_turned, 1)

        @block.scalar
        def _(act):
            act.dma_start(const[:], table[:, 0:N_CONST]).then_inc(const_in, 16)
            act.dma_start(xs_tok, x_sample[:, 0, :]).then_inc(const_in, 16)
            for dst, src in vector_sources()[6:]:
                act.dma_start(dst, src).then_inc(vectors_in, 16)
            act.dma_start(ws_nat, gmlp_w_s[0].rearrange("g i j -> i g j")).then_inc(ws_in, 16)
            act.dma_start(bs_all[:], gmlp_b_s[0].partition_broadcast(P)).then_inc(ws_in, 16)
            with nc.allow_non_contiguous_dma("a few hundred words"):
                act.dma_start(bs_first[:], gmlp_b_s[0][:, 0].partition_broadcast(P)).then_inc(ws_in, 16)
                act.dma_start(ws_first[:], gmlp_w_s[0][:, 0, 0].partition_broadcast(P)).then_inc(ws_in, 16)

            def split_ahead(n0, i, s, t):
                act.wait_ge(raw_in[1 - s], 16 * (i + n0 // 2 + 1 + s))
                act.wait_ge(tile_done, t + 4 * i + 2 * s)
                nc.scalar.activation(w_hi[:, 1 - s, :], raw[:, 1 - s, :], ACT.Copy).then_inc(hi_done, 1)

            def squares(src, m, before):
                if before >= 2:
                    act.wait_ge(sum_done, before - 1)
                nc.scalar.activation(square[:, m:m + 1, :], src, ACT.Square).then_inc(square_done, 1)

            def norm_tile(norm, k, e, sums):
                act.wait_ge(evac_done, e)
                nc.scalar.activation(xg_hi[:, k, :], x[:, k, :], ACT.Copy,
                                     scale=gain[:, norm, k:k + 1]).then_inc(xg_hi_done, 1)
                squares(x[:, k:k + 1, :], k % 2, sums + k)

            def rms_root(at):
                act.wait_ge(rms_mm, at.rms + 1)
                nc.scalar.activation(halves(root[:, :]), side[:, 0:2, 0:HALF], ACT.Sqrt, scale=1.0 / D,
                                     bias=eps[:, 0:1]).then_inc(root_done, 1)

            def down(at, n, t, e, final):
                for i in range(4):
                    if n + i < last_chunk:
                        split_ahead(n, i // 2, i % 2, t)
                    for m in range(2):
                        if not final:
                            norm_tile(at.norm, 2 * i + m, e + 2 * i + m + 1, at.sums - KD)

            def ffn(at, after, final=False):
                n, t, e, h, a = at.chunk, at.tile, at.evac, at.h, at.act
                for g, pairs in enumerate(FF_GROUPS):
                    def gate_up(i, first=False, n=n, t=t, e=e, h=h):
                        split_ahead(n, i, 0, t)
                        if first:
                            rms_root(at)
                        for m in range(2):
                            act.wait_ge(evac_done, e + 4 * i + m + 1)
                            nc.scalar.activation(tmp_act[:, m, :], tmp_in[:, m, :], ACT.Silu).then_inc(act_done, 1)
                        split_ahead(n, i, 1, t)
                        for m in range(2):
                            act.wait_ge(evac_done, e + 4 * i + m + 3)
                            act.wait_ge(eps_set, 1)
                            nc.scalar.activation(h_hi[:, bass.ds(2 * i + m, 1), :], tmp_h[:, m:m + 1, :],
                                                 ACT.Copy).then_inc(h_hi_done, 1)
                    start = 1 if g == 0 else 0
                    if start:
                        gate_up(0, True)
                    with act.Fori(0, pairs - start) as i:
                        gate_up(i + start)
                    n, t, e = n + 2 * pairs, t + 4 * pairs, e + 4 * pairs
                    if g + 1 < len(FF_GROUPS):
                        with act.Fori(0, 2) as i:
                            for s in range(2):
                                split_ahead(n, i, s, t)
                    else:
                        down(after, n, t, e, final)
                    n, t, e = n + 4, t + 8, e + 8

            act.wait_ge(eps_set, 1)
            for k in range(KD):
                norm_tile(0, k, k + 1, 0)
                if KD // 2 - 1 <= k <= KD - 2:
                    if k == KD // 2 - 1:
                        act.wait_ge(raw_in[0], 16)
                    at = slice((k - KD // 2 + 1) * SLOT // 4, (k - KD // 2 + 2) * SLOT // 4)
                    a = nc.scalar.activation(w_hi[:, 0, at], raw[:, 0, at], ACT.Copy)
                    if k == KD - 2:
                        a.then_inc(hi_done, 1)
            ffn(at_ffn[0], at_gmlp)

            n, t, e, a, sums = at_gmlp.chunk, at_gmlp.tile, at_gmlp.evac, at_gmlp.act, at_gmlp.sums

            def v_chunk(i, s, first=False):
                split_ahead(n, i, s, t)
                if first:
                    rms_root(at_gmlp)
                for m in range(2):
                    j = 4 * i + 2 * s + m
                    act.wait_ge(evac_done, e + j + 1)
                    nc.scalar.activation(v[:, bass.ds(j, 1), :], tmp_in[:, m:m + 1, :], ACT.Gelu_apprx_tanh,
                                         bias=b_in[:, bass.ds(j + GT, 1)]).then_inc(act_done, 1)
                    act.wait_ge(act_done, a + j + 1)
                    squares(v[:, bass.ds(j, 1), :], m, sums + j)
            for c in range(n_v):
                v_chunk(c // 2, c % 2, c == 0)
                if c == 0:
                    act.wait_ge(ws_turned, 1)
                    nc.scalar.activation(ws_t[:, :, :].rearrange("p (a b) c -> p a (b c)", a=2), side[:, 2:4, :],
                                         ACT.Copy).then_inc(ws_copied, 1)
            n, t, e, a = n + n_v, t + 2 * n_v, e + 2 * n_v, a + GT
            for g in range(NG):
                if g == NG // 2:
                    for i in range(4):
                        split_ahead(n, i // 2, i % 2, t)
                    n, t, e = n + 4, t + 8, e + 8
                split_ahead(n - g % 2, 0, g % 2, t - 2 * (g % 2))
                if g == 0:
                    act.wait_ge(rms_mm, at_gmlp.rms + 2)
                    nc.scalar.activation(rv_root[:, 0:QB + NS], side[:, 2, 0:QB + NS], ACT.Sqrt, scale=1.0 / GM,
                                         bias=eps[:, 0:1])
                    nc.scalar.activation(rv_root[0:NS, QB + NS:QB + NS + 1], side[0:NS, 2, QB + NS:QB + NS + 1],
                                         ACT.Sqrt, scale=1.0 / GM, bias=eps[0:NS, 0:1]).then_inc(root_done, 1)
                for m in range(2):
                    j = 2 * g + m
                    act.wait_ge(evac_done, e + m + 1)
                    if g > 0:
                        act.wait_ge(mul_done, at_gmlp.h + j - 1)
                    nc.scalar.activation(tmp_act[:, m, :], tmp_in[:, m, :], ACT.Gelu_apprx_tanh,
                                         bias=b_in[:, j:j + 1]).then_inc(act_done, 1)
                for m in range(2):
                    j = 2 * g + m
                    act.wait_ge(mul_done, at_gmlp.h + j + 1)
                    nc.scalar.activation(h_hi[:, j % KC, :], tmp_h[:, m, :], ACT.Copy).then_inc(h_hi_done, 1)
                n, t, e = n + 1, t + 2, e + 2
            down(at_ffn[1], n, t, e, False)
            ffn(at_ffn[1], at_ffn[2])
            ffn(at_ffn[2], at_mla)

            def split_part(n, tiles, i):
                if i == 0:
                    act.wait_ge(uq_rope_in[n % 2], 48 * ((n - at_uq.chunk) // 2 + 1))
                    act.wait_ge(raw_in[n % 2], 16 * (n // 2 + 1))
                    act.wait_ge(tile_done, tiles)
                at = slice(i * THIRD, (i + 1) * THIRD)
                a = nc.scalar.activation(w_hi[:, n % 2, at], raw[:, n % 2, at], ACT.Copy)
                if i == 2:
                    a.then_inc(hi_done, 1)

            def split_next(n, tiles):
                if at_uq.chunk <= n < at_wo.chunk:
                    act.wait_ge(uq_rope_in[n % 2], 48 * ((n - at_uq.chunk) // 2 + 1))
                act.wait_ge(raw_in[n % 2], 16 * (n // 2 + 1))
                act.wait_ge(tile_done, tiles)
                nc.scalar.activation(w_hi[:, n % 2, :], raw[:, n % 2, :], ACT.Copy).then_inc(hi_done, 1)

            n, t, e = at_mla.chunk, at_mla.tile, at_mla.evac
            act.wait_ge(dkv_rope_in, 16)
            split_next(n + 1, t)
            rms_root(at_mla)
            for m in range(2):
                act.wait_ge(evac_done, e + m + 1)
                nc.scalar.activation(square[:, m, :], cq[:, m, :], ACT.Square).then_inc(cq_squared, 1)
            split_next(n + 2, t + 2)
            act.wait_ge(rms_mm, at_mla.rms + 2)
            nc.scalar.activation(halves(root[:, :]), side[:, 0:2, 0:HALF], ACT.Sqrt, scale=1.0 / QL,
                                 bias=eps[:, 0:1]).then_inc(root_done, 1)
            act.wait_ge(evac_done, e + 3)
            nc.scalar.activation(tq[:, 0, :], c_t[:], ACT.Square).then_inc(c_squared, 1)
            for m in range(2):
                act.wait_ge(cqn_set, m + 1)
                nc.scalar.activation(h_hi[:, m, :], cq[:, m, :], ACT.Copy).then_inc(h_hi_done, 1)
            act.wait_ge(rms_mm, at_mla.rms + 3)
            act.wait_ge(rstd_done, at_mla.rms + 2)
            nc.scalar.activation(halves(root[:, :]), side[:, 2:4, 0:HALF], ACT.Sqrt, scale=1.0 / KL,
                                 bias=eps[:, 0:1]).then_inc(root_done, 1)

            n, t, e = at_uq.chunk, at_uq.tile, at_uq.evac
            act.wait_ge(gg_set, 1)
            for u in range(24):
                c, part = u // 6, u % 6
                if part < 3 and c < 3:
                    split_part(n + c + 1, t + 6 * c, part)
                if u >= 2:
                    act.wait_ge(q_ssq, u - 1)
                act.wait_ge(evac_done, e + u + 1)
                nc.scalar.activation(sq_h[:, u % 2, :], tq[:, u % 2, :], ACT.Square).then_inc(tq_squared, 1)
                if part % 3 != 2:
                    nc.scalar.activation(qn[:, 4 * c + 2 * (part // 3) + part % 3, :], tq[:, u % 2, :], ACT.Copy,
                                         scale=gg[:, 0:1]).then_inc(tq_read, 1)
                else:
                    nc.scalar.activation(few[0:1, 0:1], eps[0:1, 0:1], ACT.Copy).then_inc(tq_read, 1)
            act.wait_ge(q_ssq, 24)
            act.wait_ge(kr_set, 1)
            nc.scalar.activation(sq_h[:, 0, :], kr_t[:], ACT.Square).then_inc(kr_squared, 1)
            for h in range(H):
                act.wait_ge(wuk_turned, h + 1)
                if h >= 2:
                    act.wait_ge(lat_done, h - 1)
                nc.scalar.activation(wuk_t[:, h % 2, :], side[:, h % 2, 0:P], ACT.Copy).then_inc(wuk_copied, 1)
                act.wait_ge(kn_done, h + 1)
                if h >= 2:
                    act.wait_ge(k_ssq, h - 1)
                nc.scalar.activation(halves(sq_h[:, h % 2, :]), main[:, 0, :, 0:HALF], ACT.Square).then_inc(kn_squared, 1)
            for i in range(2):
                act.wait_ge(ssq_set, i + 1)
                if i:
                    act.wait_ge(scale_set, 1)
                nc.scalar.activation(root[:, 0:QB * H], ssq[:, 0:QB * H], ACT.Sqrt, scale=1.0 / QK, bias=eps[:, 0:1])
                nc.scalar.activation(root[0:NS, QB * H:5 * H], ssq[0:NS, QB * H:5 * H], ACT.Sqrt, scale=1.0 / QK,
                                     bias=eps[0:NS, 0:1]).then_inc(ssq_root, 1)
            act.wait_ge(ks_rows_turned, 1)
            nc.scalar.activation(ks_hi[:], main[0:H, 1, 1, :], ACT.Copy).then_inc(ks_hi_set, 1)
            for k in range(2 * NS):
                if k == 2 * NS - 2:
                    act.wait_ge(ks_turned, 1)
                    nc.scalar.activation(ks_all[:, :, :].rearrange("p (a b) c -> p a (b c)", a=2), main[:, 1, :, :],
                                         ACT.Copy).then_inc(ks_copied, 1)
                act.wait_ge(nat_turned, 2 * k + 2)
                if k >= 4:
                    act.wait_ge(nat_used, 2 * (k // 2) - 2)
                lo = ROPE * (k % 2)
                nc.scalar.activation(kt[lo:lo + ROPE, k // 2 % 2, 1, :], side[0:ROPE, 2 * (k % 2) + 1, :],
                                     ACT.Copy).then_inc(kt_r_copied, 1)
            act.wait_ge(sd_max, 2)
            nc.scalar.activation(sd[:, 0:PAST], sd[:, 0:PAST], ACT.Exp, bias=few[:, 1:2], scale=few[:, 10:11], accum_out=few[:, 2:3])
            nc.scalar.activation(sd[:, PAST:PAST + NS], s_new, ACT.Exp, bias=few[:, 1:2], scale=few[:, 10:11],
                                 accum_out=few[:, 13:14]).then_inc(sd_exp, 1)

            n = at_wo.chunk
            for h in range(H + 1):
                g = h - 1
                if g >= 0:
                    act.wait_ge(prob_turned, 3 * g + 1)
                    nc.scalar.activation(prob_t[:, 0:4 * P], side[:, 2, :], ACT.Copy).then_inc(prob_t_act, 1)
                    act.wait_ge(prob_turned, 3 * g + 3)
                    nc.scalar.activation(prob_t[:, 8 * P:10 * P], side[:, 1, 0:2 * P], ACT.Copy).then_inc(prob_t_act, 1)
                else:
                    act.wait_ge(sd_turned, 1)
                    nc.scalar.activation(ks_all[:, :, :].rearrange("p (a b) c -> p a (b c)", a=2), side[:, 2:4, :],
                                         ACT.Copy).then_inc(sd_t_copied, 1)
                if h < H:
                    act.wait_ge(max_done, h + 1)
                    if h >= 1:
                        act.wait_ge(inv_done, h)
                    for q in range(QB):
                        nc.scalar.activation(prob[:, P_AT[q] * P:(P_AT[q] + q + 1) * P],
                                                 main[:, q // 2, q % 2, 0:(q + 1) * P], ACT.Exp,
                                                 bias=few[:, 4 + q:5 + q], scale=rq[:, q * H + h:q * H + h + 1],
                                                 accum_out=few[:, 12 + q:13 + q]).then_inc(exp_done, 1)
                if h == 0:
                    act.wait_ge(pv_summed, 1)
                    nc.scalar.activation(o_rows.rearrange("p (a b) c -> p a (b c)", a=2), side[0:H, 2:4, :],
                                         ACT.Copy).then_inc(o_rows_set, 1)
                if g >= 0:
                    act.wait_ge(uv_copied, g + 1)
                    nc.scalar.activation(h_hi[:, g % KC, :], square[:, g % 2, :], ACT.Copy).then_inc(h_hi_done, 1)
                if h == 2:
                    split_next(n, at_uq.tile + 18)
                if g == KC - 1:
                    for i in range(4):
                        split_next(n + i + 1, at_wo.tile + 2 * i)
                    n += 4
            down(at_ffn[3], n, at_wo.tile + 8, at_wo.evac + 8, False)
            ffn(at_ffn[3], at_end, True)
            for k in range(KD):
                act.wait_ge(out_turned, k + 1)
                nc.scalar.activation(x_tok[:, :, k * P:(k + 1) * P], side[:, k % 2, :].rearrange("p (q c) -> p q c", q=QB),
                                     ACT.Copy)
                nc.scalar.activation(xs_tok[:, k * P:(k + 1) * P], side[0:NS, 2 + k % 2, 0:P],
                                     ACT.Copy).then_inc(out_copied, 1)

        @block.vector
        def _(dve):
            def split_ahead(n0, i, s):
                dve.wait_ge(hi_done, n0 + 2 * i + s + 2)
                nc.vector.tensor_tensor(w_lo[:, 1 - s, :], raw[:, 1 - s, :], w_hi[:, 1 - s, :].bitcast(F32),
                                        ALU.subtract).then_inc(lo_done, 1)

            def rstd(at):
                dve.wait_ge(root_done, at.rms + 1)
                nc.vector.reciprocal(rstd_all[:], root[:]).then_inc(rstd_done, 1)
                dve.wait_ge(rstd_done, at.rms + 1)

            def norm_tile(norm, k):
                dve.wait_ge(xg_hi_done, KD * norm + k + 1)
                nc.vector.scalar_tensor_tensor(xg_lo[:, k, :], x[:, k, :], gain[:, norm, k:k + 1],
                                               xg_hi[:, k, :].bitcast(F32), ALU.mult, ALU.subtract).then_inc(xg_lo_done, 1)

            def scaled(m, t):
                dve.wait_ge(tile_done, t)
                nc.vector.tensor_tensor(halves(tmp_in[:, m, :]), main[:, m, :, 0:HALF], halves(rstd_all[:, :]),
                                        ALU.mult).then_inc(evac_done, 1)

            def add_to_x(k, m, t, scale):
                dve.wait_ge(tile_done, t)
                xk = x[:, bass.ds(k, 1), :].rearrange("p a (h n) -> p (a h) n", h=2)
                nc.vector.scalar_tensor_tensor(xk, main[:, m, :, 0:HALF], scale, xk, ALU.mult, ALU.add).then_inc(evac_done, 1)

            def down(at, n, t, scale, final):
                for i in range(4):
                    if n + i < last_chunk:
                        split_ahead(n, i // 2, i % 2)
                    for m in range(2):
                        add_to_x(2 * i + m, m, t + 2 * i + m + 1, scale)
                        if not final:
                            norm_tile(at.norm, 2 * i + m)

            def down_loop(n, t, scale):
                with dve.Fori(0, 2) as i:
                    for s in range(2):
                        split_ahead(n, i, s)
                        for m in range(2):
                            add_to_x(4 * i + 2 * s + m, m, t + 4 * i + 2 * s + m + 1, scale)

            def ffn(at, after, final=False):
                n, t, h = at.chunk, at.tile, at.mul
                for g, pairs in enumerate(FF_GROUPS):
                    def gate_up(i, first=False, n=n, t=t, h=h):
                        split_ahead(n, i, 0)
                        if first:
                            rstd(at)
                        for m in range(2):
                            scaled(m, t + 4 * i + m + 1)
                        split_ahead(n, i, 1)
                        for m in range(2):
                            dve.wait_ge(tile_done, t + 4 * i + m + 3)
                            dve.wait_ge(mul_done, h + 2 * i + m + 1)
                            nc.vector.tensor_tensor(halves(tmp_h[:, m, :]), main[:, m, :, 0:HALF],
                                                    halves(tmp_mul[:, m, :]), ALU.mult).then_inc(evac_done, 1)
                    start = 1 if g == 0 else 0
                    if start:
                        gate_up(0, True)
                    with dve.Fori(0, pairs - start) as i:
                        gate_up(i + start)
                    n, t, h = n + 2 * pairs, t + 4 * pairs, h + 2 * pairs
                    if g + 1 < len(FF_GROUPS):
                        down_loop(n, t, 0.5)
                    else:
                        down(after, n, t, 0.5, final)
                    n, t = n + 4, t + 8

            nc.vector.memset(eps[:], EPS).then_inc(eps_set, 1)
            dve.wait_ge(vectors_turned, 1)
            nc.vector.tensor_copy(vectors[:, 0:n_vec], side[:, 0, 0:n_vec]).then_inc(vectors_set, 1)
            dve.wait_ge(vectors_set, 1)
            for k in range(KD):
                dve.wait_ge(tile_done, k + 1)
                nc.vector.tensor_copy(x[:, k, 0:SEQ], main[:, k % 2, 0, :])
                nc.vector.tensor_copy(x[:, k, SEQ:TOK], main[:, k % 2, 1, 0:NS]).then_inc(evac_done, 1)
                if k:
                    norm_tile(0, k - 1)
            dve.wait_ge(hi_done, 1)
            nc.vector.tensor_tensor(w_lo[:, 0, :], raw[:, 0, :], w_hi[:, 0, :].bitcast(F32),
                                    ALU.subtract).then_inc(lo_done, 1)
            norm_tile(0, KD - 1)
            ffn(at_ffn[0], at_gmlp)

            n, t, a = at_gmlp.chunk, at_gmlp.tile, at_gmlp.act

            def v_chunk(i, s, first=False):
                split_ahead(n, i, s)
                if first:
                    rstd(at_gmlp)
                for m in range(2):
                    j = 4 * i + 2 * s + m
                    if not isinstance(j, int) or j >= 2:
                        dve.wait_ge(act_done, a + j - 1)
                    scaled(m, t + j + 1)
            v_chunk(0, 0, True)
            v_chunk(0, 1)
            with dve.Fori(0, n_v // 2 - 1) as i:
                v_chunk(i + 1, 0)
                v_chunk(i + 1, 1)
            n, t, a = n + n_v, t + 2 * n_v, a + GT

            def v_times_gain(g):
                vg = v[:, 2 * g:2 * g + 2, :]
                nc.vector.tensor_tensor(vg, vg, bc(v_gain[:, 2 * g:2 * g + 2], TOK), ALU.mult).then_inc(vg_done, 2)

            dve.wait_ge(square_done, at_gmlp.sums + GT)
            v_times_gain(0)
            for g in range(NG):
                if g == NG // 2:
                    down_loop(n, t, 1.0)
                    n, t = n + 4, t + 8
                split_ahead(n - g % 2, 0, g % 2)
                if g == 0:
                    dve.wait_ge(root_done, at_gmlp.rms + 2)
                    nc.vector.reciprocal(rv[:, 0:QB + NS], rv_root[:, 0:QB + NS])
                    nc.vector.reciprocal(rv[0:NS, QB + NS:QB + NS + 1],
                                         rv_root[0:NS, QB + NS:QB + NS + 1]).then_inc(rstd_done, 1)
                    dve.wait_ge(rstd_done, at_gmlp.rms + 2)
                dve.wait_ge(v_turned, g + 1)
                for m in range(2):
                    nc.vector.tensor_tensor(v_tok[:, m, :, :], side[:, m, :].rearrange("p (q c) -> p q c", q=QB),
                                            bc(rv[:, 0:QB], P), ALU.mult).then_inc(v_copied, 1)
                if g >= 2:
                    dve.wait_ge(vs_out[g % 2], 16 * (g // 2))
                nc.vector.tensor_scalar(vs_tok[:, g % 2, :, :], side[0:NS, 2, 0:2 * P].rearrange("p (m c) -> p m c", m=2),
                                        rv[0:NS, QB + NS:QB + NS + 1], None, ALU.mult).then_inc(v_seen, 1)
                dve.wait_ge(vg_done, 2 * g + 2)
                if g > 0:
                    dve.wait_ge(mul_done, at_gmlp.h + 2 * g)
                sm = tmp_mul[:, :, SEQ:TOK]
                nc.vector.scalar_tensor_tensor(sm, v[:, 2 * g:2 * g + 2, SEQ:TOK], ws_first[:, g:g + 1],
                                               rv[:, QB:QB + NS].unsqueeze(1).to_broadcast([P, 2, NS]),
                                               ALU.mult, ALU.mult).then_inc(sample_mix, 1)
                dve.wait_ge(sample_mix, g + 1)
                nc.vector.tensor_scalar(sm, sm, bs_first[:, g:g + 1], None, ALU.add)
                if g + 1 < NG:
                    v_times_gain(g + 1)
                for m in range(2):
                    dve.wait_ge(act_done, a + 2 * g + m - 1)
                    scaled(m, t + m + 1)
                for m in range(2):
                    dve.wait_ge(mix_done, 2 * g + m + 1)
                    bank = (3, 0)[m]
                    nc.vector.tensor_tensor(tmp_mul[:, m, 0:SEQ].rearrange("p (q c) -> p q c", q=QB),
                                            side[:, bank, :].rearrange("p (q c) -> p q c", q=QB),
                                            bs_all[:, g:g + 1, :].to_broadcast([P, QB, P]), ALU.add).then_inc(mixed, 1)
                n, t = n + 1, t + 2
            down(at_ffn[1], n, t, 1.0, False)
            ffn(at_ffn[1], at_ffn[2])
            ffn(at_ffn[2], at_mla)

            def split_next(n):
                dve.wait_ge(hi_done, n + 1)
                nc.vector.tensor_tensor(w_lo[:, n % 2, :], raw[:, n % 2, :], w_hi[:, n % 2, :].bitcast(F32),
                                        ALU.subtract).then_inc(lo_done, 1)

            def scaled_to(dst, m, t):
                dve.wait_ge(tile_done, t)
                nc.vector.tensor_tensor(halves(dst), main[:, m, :, 0:HALF], halves(rstd_all[:, :]),
                                        ALU.mult).then_inc(evac_done, 1)

            n, t = at_mla.chunk, at_mla.tile
            split_next(n + 1)
            rstd(at_mla)
            nc.vector.tensor_tensor(gg[:, 0:1], nope_gains[:, 0:1], nope_gains[:, 1:2], ALU.mult)
            nc.vector.tensor_tensor(gg[:, 1:2], rope_gains[:, 0:1], rope_gains[:, 1:2], ALU.mult).then_inc(gg_set, 1)
            scaled_to(cq[:, 0, :], 0, t + 1)
            scaled_to(cq[:, 1, :], 1, t + 2)
            split_next(n + 2)
            scaled_to(c_t[:, :], 0, t + 3)
            inv = square_sum
            dve.wait_ge(root_done, at_mla.rms + 2)
            nc.vector.reciprocal(inv[:], root[:]).then_inc(rstd_done, 1)
            dve.wait_ge(rstd_done, at_mla.rms + 2)
            for m in range(2):
                nc.vector.scalar_tensor_tensor(cq[:, m, :], cq[:, m, :], q_gain[:, m:m + 1], inv[:], ALU.mult,
                                               ALU.mult).then_inc(cqn_set, 1)
            scaled_to(kr_raw, 1, t + 4)

            def k_parts(i):
                if i == 0:
                    dve.wait_ge(kv_in, 32)
                    dve.wait_ge(kr_swapped, 1)
                    nc.vector.tensor_tensor(halves(rope_b[:, :]), side[:, 0:2, 0:HALF], halves(trig[:, 1, :]),
                                            ALU.mult).then_inc(rope_b_set, 1)
                    nc.vector.tensor_tensor(kr_t[:], kr_raw, trig[:, 0, :], ALU.mult).then_inc(kr_part, 1)
                    dve.wait_ge(rope_b_set, 1)
                    dve.wait_ge(kr_part, 1)
                    nc.vector.tensor_tensor(kr_t[:], kr_t[:], rope_b[:], ALU.add).then_inc(kr_set, 1)
                elif i == 1:
                    dve.wait_ge(gg_set, 1)
                    nc.vector.tensor_scalar(trig_g[:], trig[:], gg[:, 1:2], None, ALU.mult).then_inc(trig_set, 1)
                elif 3 <= i <= 6:
                    if i == 3:
                        dve.wait_ge(root_done, at_mla.rms + 3)
                        dve.wait_ge(cqn_set, 2)
                    at = slice((i - 3) * TOK // 4, (i - 2) * TOK // 4)
                    a = nc.vector.reciprocal(inv[:, at], root[:, at])
                    if i == 6:
                        a.then_inc(rstd_done, 1)
                elif i == 7:
                    dve.wait_ge(rstd_done, at_mla.rms + 3)
                    nc.vector.scalar_tensor_tensor(c_t[:], c_t[:], kv_gain, inv[:], ALU.mult, ALU.mult).then_inc(c_set, 1)

            n, t = at_uq.chunk, at_uq.tile
            for u in range(24):
                c, part = u // 6, u % 6
                if part >= 3 and c < 3:
                    dve.wait_ge(hi_done, n + c + 2)
                    at = slice((part - 3) * THIRD, (part - 2) * THIRD)
                    s = (n + c + 1) % 2
                    a = nc.vector.tensor_tensor(w_lo[:, s, at], raw[:, s, at], w_hi[:, s, at].bitcast(F32), ALU.subtract)
                    if part == 5:
                        a.then_inc(lo_done, 1)
                if u >= 2:
                    dve.wait_ge(tq_read, u - 1)
                    if (u - 2) % 3 == 2:
                        dve.wait_ge(rope_a_set, (u - 2) // 3 + 1)
                dve.wait_ge(tile_done, t + u + 1)
                nc.vector.tensor_copy(halves(tq[:, u % 2, :]), main[:, u % 2, :, 0:HALF]).then_inc(evac_done, 1)
                if part % 3 == 2:
                    r_ = 2 * c + part // 3
                    dve.wait_ge(swapped, r_ + 1)
                    if r_ >= 1:
                        dve.wait_ge(qr_set, r_)
                    else:
                        dve.wait_ge(kr_set, 1)
                        dve.wait_ge(trig_set, 1)
                    nc.vector.tensor_tensor(halves(rope_b[:, :]), side[:, 0:2, 0:HALF], halves(trig_g[:, 1, :]),
                                            ALU.mult).then_inc(rope_b_set, 1)
                k_parts(u)
            for b in range(QB + 1):
                w = P if b < QB else NS
                dve.wait_ge(row_turned, b + 1)
                dst = rows[:, b, :] if b < QB else rows_s[:, :]
                nc.vector.tensor_copy(dst[:, 0:KL + ROPE], side[0:w, b % 2, 0:KL + ROPE]).then_inc(row_copied, 1)

            def scales(i, bank, extra):
                if i:
                    dve.wait_ge(ssq_root, 1)
                for r0, r1, a, b in ((0, P, 0, QB * H), (0, NS, QB * H, 5 * H)):
                    nc.vector.tensor_copy(extra(r0, r1, a, b)[0], extra(r0, r1, a, b)[1]).then_inc(rope_part, 1)
                dve.wait_ge(rope_part, 4 * i + 2)
                for r0, r1, a, b in ((0, P, 0, QB * H), (0, NS, QB * H, 5 * H)):
                    nb = (b - a) // H
                    other = ssq[r0:r1, a:b].rearrange("p (b h) -> p b h", h=H) if i == 0 else bc(krq[r0:r1, a // H:b // H], H)
                    nc.vector.tensor_tensor(ssq[r0:r1, a:b].rearrange("p (b h) -> p b h", h=H),
                                            side[r0:r1, bank, a:b].rearrange("p (b h) -> p b h", h=H), other,
                                            ALU.add).then_inc(rope_part, 1)

            def scales_end(i, dst):
                dve.wait_ge(ssq_root, i + 1)
                nc.vector.reciprocal(dst[:, 0:QB * H], root[:, 0:QB * H])
                nc.vector.reciprocal(dst[0:NS, QB * H:5 * H], root[0:NS, QB * H:5 * H]).then_inc(scale_set, 1)
                dve.wait_ge(scale_set, i + 1)

            dve.wait_ge(q_ssq, 24)
            scales(0, 2, lambda r0, r1, a, b: (ssq[r0:r1, a:b], side[r0:r1, 2, 5 * H + a:5 * H + b]))
            dve.wait_ge(rope_part, 4)
            nc.vector.tensor_copy(few[:, 23:24], eps[:]).then_inc(ssq_set, 1)
            for h in range(H):
                dve.wait_ge(lat_done, h + 1)
                nc.vector.tensor_copy(halves(qn[:, h, :]), main[:, 1, :, 0:HALF]).then_inc(lat_copied, 1)
            scales_end(0, rq)
            nc.vector.tensor_scalar(rq[:, 0:QB * H], rq[:, 0:QB * H], QK ** -0.5, None, ALU.mult)
            nc.vector.tensor_scalar(rq[0:NS, QB * H:5 * H], rq[0:NS, QB * H:5 * H], QK ** -0.5, None,
                                    ALU.mult).then_inc(q_ssq_read, 1)
            dve.wait_ge(k_ssq, H)
            scales(1, 3, lambda r0, r1, a, b: (krq[r0:r1, a // H:b // H], side[r0:r1, 3, 5 * H + a // H:5 * H + b // H]))
            dve.wait_ge(rope_part, 8)
            nc.vector.tensor_copy(few[:, 23:24], eps[:]).then_inc(ssq_set, 1)
            scales_end(1, ks)
            nc.vector.tensor_copy(rows[:, :, KL + ROPE:CD], ks[:, 0:QB * H].rearrange("p (b h) -> p b h", h=H))
            nc.vector.tensor_copy(rows_s[:, KL + ROPE:CD], ks[0:NS, QB * H:5 * H]).then_inc(rows_done, 1)
            nc.vector.tensor_copy(pick[:], ident[0:H, 0:H])
            nc.vector.tensor_copy(mask_ops[:, 0, :], ident)
            nc.vector.tensor_copy(mask_ops[:, 1, :], causal)
            dve.wait_ge(lat_copied, H)
            dve.wait_ge(qr_set, H // 2)
            nc.vector.tensor_copy(q_all[:, 0, :].rearrange("p (b h) -> p b h", h=H),
                                  qn[:, :, SEQ:TOK].rearrange("p h b -> p b h")).then_inc(q_all_set, 1)
            for odd in range(2):
                lo = ROPE * odd
                nc.vector.tensor_copy(
                    q_all[0:ROPE, 1, :].rearrange("p (b g t) -> p b g t", g=H // 2, t=2)[:, :, :, odd],
                    qr[lo:lo + ROPE, :, SEQ:TOK].rearrange("p g b -> p b g")).then_inc(q_all_set, 1)
            dve.wait_ge(q_all_set, 3)
            dve.wait_ge(qpad_zero, 1)
            for b in range(NS):
                nc.vector.tensor_copy(q_pad[:, 0, b, b * H:(b + 1) * H], q_all[:, 0, b * H:(b + 1) * H])
                lo = ROPE * (b % 2)
                a = nc.vector.tensor_copy(q_pad[lo:lo + ROPE, 1, b // 2, b * H:(b + 1) * H],
                                          q_all[0:ROPE, 1, b * H:(b + 1) * H])
            a.then_inc(q_pad_set, 1)
            dve.wait_ge(q_ssq_read, 1)
            nc.vector.tensor_copy(ks_new[:, 0, :].rearrange("p (b h) -> p b h", h=H),
                                  ks[0:NS, QB * H:5 * H].unsqueeze(1).to_broadcast([NS, NS, H])).then_inc(ks_new_set, 1)
            nc.vector.tensor_tensor(ks_new[:, 1, :].rearrange("p (b h) -> p b h", h=H),
                                    own_rows.rearrange("p (b h) -> p b h", h=H),
                                    rq[0:NS, QB * H:5 * H].unsqueeze(1).to_broadcast([NS, NS, H]),
                                    ALU.mult).then_inc(ks_new_set, 1)

            def scale_keys(h, bank=side[:, 0, :]):
                dve.wait_ge(scales_spread, h + 1)
                if h >= 2:
                    dve.wait_ge(scored, h - 1)
                nc.vector.tensor_tensor(cks[:, h % 2, :], bank, c_t[:, 0:SEQ], ALU.mult).then_inc(c_scaled, 1)
                nc.vector.tensor_tensor(krs[:, h % 2, :], bank, kr_t[:, 0:SEQ], ALU.mult).then_inc(kr_scaled, 1)

            for k in range(2 * NS):
                if k == NS // 2 + 2:
                    scale_keys(0, main[:, 1, 0, :])
                if k == 1:
                    dve.wait_ge(new_scored, 1)
                    nc.vector.tensor_copy(few[:, 10:11], main[:, 1, 0, 2 * NS:2 * NS + 1])
                    nc.vector.tensor_copy(krq_s, main[:, 1, 0, NS:2 * NS]).then_inc(new_ready, 1)
                    dve.wait_ge(new_ready, 1)
                    nc.vector.tensor_tensor(s_new, main[:, 1, 0, 0:NS], krq_s, ALU.mult).then_inc(new_ready, 1)
                    nc.vector.tensor_scalar(few[:, 11:12], few[:, 10:11], -1.0, None, ALU.mult)
                    dve.wait_ge(new_ready, 2)
                    nc.vector.tensor_tensor(s_new, s_new, own, ALU.add).then_inc(sd_set, 1)
                    dve.wait_ge(sd_set, 1)
                    nc.vector.tensor_reduce(few[:, 9:10], s_new, AX.X, ALU.max).then_inc(sd_max, 1)
                    dve.wait_ge(ks_hi_set, 1)
                    nc.vector.tensor_tensor(ks_lo[:], main[0:H, 1, 1, :], ks_hi[:].bitcast(F32),
                                            ALU.subtract).then_inc(ks_lo_set, 1)
                dve.wait_ge(nat_turned, 2 * k + 1)
                if k >= 2:
                    dve.wait_ge(nat_used, k - 1)
                nc.vector.tensor_copy(kt[:, k % 2, 0, :], side[:, 2 * (k % 2), :]).then_inc(kt_c_copied, 1)
            dve.wait_ge(nat_used, 2 * NS)
            dve.wait_ge(ks_copied, 1)
            nc.vector.tensor_tensor(sd[:, 0:PAST].rearrange("p (a c) -> p a c", a=2), main[:, 0, :, :],
                                    ks_all[:, :, :].rearrange("p (a b) c -> p a (b c)", a=2), ALU.mult).then_inc(sd_set, 1)
            dve.wait_ge(sd_set, 2)
            nc.vector.tensor_reduce(few[:, 0:1], sd[:, 0:PAST], AX.X, ALU.max).then_inc(sd_set, 1)
            dve.wait_ge(sd_set, 3)
            dve.wait_ge(sd_max, 1)
            nc.vector.tensor_scalar(few[:, 1:2], few[:, 0:1], few[:, 9:10], few[:, 11:12], ALU.max,
                                    ALU.mult).then_inc(sd_max, 1)

            dve.wait_ge(sd_exp, 1)
            nc.vector.tensor_tensor(few[:, 2:3], few[:, 2:3], few[:, 13:14], ALU.add).then_inc(sd_inv, 1)
            dve.wait_ge(sd_inv, 1)
            nc.vector.reciprocal(few[:, 3:4], few[:, 2:3]).then_inc(sd_inv, 1)
            dve.wait_ge(sd_inv, 2)
            nc.vector.tensor_scalar(sd, sd, few[:, 3:4], None, ALU.mult).then_inc(sd_prob, 1)

            n = at_wo.chunk

            for h in range(H + 1):
                g = h - 1
                if h < H:
                    dve.wait_ge(scored, h + 1)
                for q in range(QB):
                    if q == 2 and g >= 0:
                        dve.wait_ge(prob_turned, 3 * g + 2)
                        if g >= 1:
                            dve.wait_ge(pv_done, g)
                        nc.vector.tensor_copy(prob_t[:, 4 * P:8 * P], side[:, 3, :]).then_inc(prob_t_dve, 1)
                    if h < H:
                        a = nc.vector.tensor_reduce(few[:, 16 + q:17 + q], main[:, q // 2, q % 2, 0:(q + 1) * P], AX.X,
                                                    ALU.max)
                if h < H:
                    a.then_inc(max_set, 1)
                    dve.wait_ge(max_set, h + 1)
                    rh = rq[:, 0:QB * H].rearrange("p (b h) -> p b h", h=H)[:, :, h]
                    nc.vector.scalar_tensor_tensor(few[:, 4:4 + QB], few[:, 16:16 + QB], -1.0, rh, ALU.mult,
                                                   ALU.mult).then_inc(max_done, 1)
                if h == 0:
                    dve.wait_ge(sd_turned, 1)
                    nc.vector.tensor_copy(p_new, side[0:NS, 1, 0:P]).then_inc(sd_t_copied, 1)
                if g >= 0:
                    dve.wait_ge(pv_done, g + 1)
                    nc.vector.tensor_copy(o_t[:, 0:SEQ], side[:, 2, :]).then_inc(o_copied, 1)
                if h + 1 < H:
                    scale_keys(h + 1)
                if h < H:
                    dve.wait_ge(exp_done, QB * (h + 1))
                    if h >= 1:
                        dve.wait_ge(prob_done, h)
                    nc.vector.reciprocal(inv_sum, few[:, 12:12 + QB]).then_inc(inv_done, 1)
                    dve.wait_ge(inv_done, h + 1)
                    for q in range(QB):
                        pq = prob[:, P_AT[q] * P:(P_AT[q] + q + 1) * P]
                        a = nc.vector.tensor_scalar(pq, pq, inv_sum[:, q:q + 1], None, ALU.mult)
                    a.then_inc(prob_done, 1)
                if h == 0:
                    dve.wait_ge(os_done, 1)
                    nc.vector.tensor_copy(o_s[:], side[:, 1, 0:P]).then_inc(os_copied, 1)
                if g >= 0:
                    dve.wait_ge(uv_done, g + 1)
                    if g >= 2:
                        dve.wait_ge(h_lo_done, at_wo.h + g - 1)
                    nc.vector.tensor_copy(square[:, g % 2, 0:SEQ], side[:, 3, :])
                    nc.vector.tensor_copy(square[:, g % 2, SEQ:TOK], side[:, 1, 0:NS]).then_inc(uv_copied, 1)
                if h == 2:
                    split_next(n)
                if g == KC - 1:
                    down_loop(n, at_wo.tile, 1.0)
                    n += 4
            down(at_ffn[3], n, at_wo.tile + 8, 1.0, False)
            ffn(at_ffn[3], at_end, True)

        @block.gpsimd
        def _(pool):
            def add_squares(m, before, first):
                pool.wait_ge(square_done, before + 1)
                if first:
                    nc.gpsimd.tensor_copy(square_sum[:], square[:, m, :]).then_inc(sum_done, 1)
                else:
                    pool.wait_ge(sum_done, before)
                    nc.gpsimd.tensor_tensor(square_sum[:], square_sum[:], square[:, m, :], ALU.add).then_inc(sum_done, 1)

            def h_rest(m, f, h):
                pool.wait_ge(h_hi_done, h)
                if not isinstance(h, int):
                    pool.wait_ge(ws_masked, 1)
                nc.gpsimd.tensor_tensor(h_lo[:, bass.ds(f, 1), :], tmp_h[:, m:m + 1, :],
                                        h_hi[:, bass.ds(f, 1), :].bitcast(F32), ALU.subtract).then_inc(h_lo_done, 1)

            def ffn(at, after, final=False):
                h, a = at.h, at.act
                for g, pairs in enumerate(FF_GROUPS):
                    with pool.Fori(0, pairs) as i:
                        for m in range(2):
                            pool.wait_ge(act_done, a + 2 * i + m + 1)
                            nc.gpsimd.tensor_tensor(tmp_mul[:, m, :], tmp_act[:, m, :], rstd_all[:],
                                                    ALU.mult).then_inc(mul_done, 1)
                        for m in range(2):
                            h_rest(m, 2 * i + m, h + 2 * i + m + 1)
                    h, a = h + 2 * pairs, a + 2 * pairs
                if not final:
                    for k in range(KD):
                        add_squares(k % 2, after.sums - KD + k, k == 0)

            for k in range(KD):
                add_squares(k % 2, k, k == 0)
            pool.wait_ge(ws_in, 16 * 4)
            nc.gpsimd.affine_select(out=ws_nat, in_=ws_nat, compare_op=ALU.is_ge, fill=0.0, base=0,
                                    pattern=[[0, NG], [-1, P]], channel_multiplier=1).then_inc(ws_masked, 1)
            ffn(at_ffn[0], at_gmlp)

            add_squares(0, at_gmlp.sums, True)
            add_squares(1, at_gmlp.sums + 1, False)
            with pool.Fori(0, GT // 2 - 1) as i:
                for m in range(2):
                    add_squares(m, at_gmlp.sums + 2 * i + 2 + m, False)
            for g in range(NG):
                pool.wait_ge(v_seen, g + 1)
                pool.dma_start(new_v[0, :, 0, 2 * g * P:2 * (g + 1) * P], vs_tok[:, g % 2, :, :].rearrange("p m c -> p (m c)"))\
                    .then_inc(vs_out[g % 2], 16)
                for m in range(2):
                    j = 2 * g + m
                    pool.wait_ge(act_done, at_gmlp.act + GT + j + 1)
                    pool.wait_ge(mixed, j + 1)
                    if g > 0:
                        pool.wait_ge(h_lo_done, at_gmlp.h + j - 1)
                    nc.gpsimd.tensor_tensor(tmp_h[:, m, :], tmp_act[:, m, :], tmp_mul[:, m, :],
                                            ALU.mult).then_inc(mul_done, 1)
                for m in range(2):
                    h_rest(m, (2 * g + m) % KC, at_gmlp.h + 2 * g + m + 1)
            for s in range(2):
                pool.wait_ge(vs_out[s], 16 * NG // 2)
            for k in range(KD):
                add_squares(k % 2, at_ffn[1].sums - KD + k, k == 0)
            ffn(at_ffn[1], at_ffn[2])
            ffn(at_ffn[2], at_mla)

            for m in range(2):
                pool.wait_ge(h_hi_done, at_mla.h + m + 1)
                nc.gpsimd.tensor_tensor(h_lo[:, m, :], cq[:, m, :], h_hi[:, m, :].bitcast(F32),
                                        ALU.subtract).then_inc(h_lo_done, 1)
            pool.wait_ge(trig_set, 1)
            pool.wait_ge(kr_set, 1)
            for r_ in range(H // 2):
                u = 3 * r_ + 2
                pool.wait_ge(evac_done, at_uq.evac + u + 1)
                if r_:
                    pool.wait_ge(qr_set, r_)
                nc.gpsimd.tensor_tensor(rope_a[:], tq[:, u % 2, :], trig_g[:, 0, :], ALU.mult).then_inc(rope_a_set, 1)
                pool.wait_ge(rope_b_set, r_ + 2)
                pool.wait_ge(rope_a_set, r_ + 1)
                nc.gpsimd.tensor_tensor(qr[:, r_, :], rope_a[:], rope_b[:], ALU.add).then_inc(qr_set, 1)
            pool.wait_ge(lat_done, H)
            pool.wait_ge(k_ssq, H)
            pool.wait_ge(qr_set, H // 2)
            nc.gpsimd.memset(q_pad[:], 0.0).then_inc(qpad_zero, 1)
            pool.wait_ge(rms_mm, at_mla.rms + 2)
            for k in range(2 * NS):
                if k % 2 == 0:
                    pool.wait_ge(nat_in[k // 2], 128)
                b, j = k // 2, 4 * (k % 2)
                a = nc.gpsimd.tensor_copy(ks_all[:, j:j + 4, b * H:(b + 1) * H], pieces[k][:, :, KL + ROPE:CD])
            a.then_inc(ks_all_set, 1)
            pool.wait_ge(os_copied, 1)
            for g in range(H):
                if g >= 1:
                    pool.wait_ge(uv_done, g)
                nc.gpsimd.tensor_copy(o_t[:, SEQ:TOK], o_s[:, :].rearrange("p (b h) -> p b h", h=H)[:, :, g])\
                    .then_inc(o_samples, 1)
                pool.wait_ge(h_hi_done, at_wo.h + g + 1)
                nc.gpsimd.tensor_tensor(h_lo[:, g % KC, :], square[:, g % 2, :], h_hi[:, g % KC, :].bitcast(F32),
                                        ALU.subtract).then_inc(h_lo_done, 1)
            for k in range(KD):
                add_squares(k % 2, at_ffn[3].sums - KD + k, k == 0)
            ffn(at_ffn[3], at_end, True)


INPUTS = ("x_prompt", "x_sample", "cache_mla", "page_table", "norm_g", "ffn_w_gate", "ffn_w_up", "ffn_w_down",
          "gmlp_w_in", "gmlp_b_in", "gmlp_v_norm", "gmlp_w_s", "gmlp_b_s", "gmlp_w_out",
          "mla_w_dq", "mla_q_norm", "mla_w_uq", "mla_w_dkv", "mla_kv_norm", "mla_w_uk", "mla_w_uv",
          "mla_qk_gain_q", "mla_qk_gain_k", "mla_w_o")
OUTPUTS = ((1, SEQ, D), (NS, 1, D), (1, 1, SEQ, CD), (1, NS, 1, CD), (1, NS, 1, GM))


def kernel(**inputs):
    import concourse.bacc as bacc
    from concourse.bass_utils import run_bass_kernel_spmd

    nc = bacc.Bacc("TRN2", target_bir_lowering=False, num_devices=1)
    arrays, args = {}, []
    for name in INPUTS:
        a = np.ascontiguousarray(inputs[name])
        arrays[f"in_{name}"] = a
        args.append(nc.dram_tensor(f"in_{name}", a.shape, mybir.dt.from_np(a.dtype), kind="ExternalInput").ap())
    for i, shape in enumerate(OUTPUTS):
        args.append(nc.dram_tensor(f"out_{i}", shape, F32, kind="ExternalOutput").ap())
    program(nc, *args)
    r = run_bass_kernel_spmd(nc, [arrays], core_ids=[0])
    return tuple(r.results[0][f"out_{i}"] for i in range(len(OUTPUTS)))
```
